# Optimizing a Trainium2 kernel written in Bass

```python
import math
import jax
import jax.numpy as jnp
from jax import lax
import numpy as np

D_MODEL = 1024
BATCH = 1
SEQ = 128
DEPTH = 2
DEC_BATCH = 1
DEC_SEQ = 256
PAST_LEN = 128

GRID_W = 64
MIX_W = D_MODEL
NA_HEADS = 8
NA_HD = MIX_W // 2 // NA_HEADS
NA_W = NA_HEADS * NA_HD
NA_KH = 8
NA_KW = 16
NA_QCB = 16
NA_KCB = 32
CTX_QBLK = 128
GDN_HEADS = 4
GDN_DK = MIX_W // 2 // GDN_HEADS
GDN_DV = GDN_DK
GDN_W = GDN_HEADS * GDN_DV
CONV_K = 5
GDN_CHUNK = 64
ROPE_BASE = 10000.0
N_GROUPS = 4
EXP_PER_GROUP = 4
N_EXPERTS = N_GROUPS * EXP_PER_GROUP
TOP_K = 2
EXPERT_FF = D_MODEL // 2
EPS = 1e-6
N_IN = 3 * NA_W + 4 * GDN_W + 4 * GDN_HEADS
SPLITS = (NA_W, 2 * NA_W, 3 * NA_W, 3 * NA_W + 3 * GDN_W, 3 * NA_W + 4 * GDN_W, 3 * NA_W + 4 * GDN_W + 2 * GDN_HEADS)

kernel_name = "hybrid_na_gdn_hmoe_diffusion_step"

F32 = jnp.float32

def rms_norm(x, g):
    xf = x.astype(F32)
    y = xf * lax.rsqrt(jnp.mean(xf * xf, axis=-1, keepdims=True) + EPS)
    return (y * g.astype(F32)).astype(x.dtype)

def l2_normalize(x):
    return x * lax.rsqrt(jnp.sum(x * x, axis=-1, keepdims=True) + EPS)

def modulation(cvec, lw):
    m = jax.nn.silu(cvec) @ lw["ada_w"] + lw["ada_b"]
    return jnp.split(m[..., None, :], 6, axis=-1)

def modulate(h, shift, scale):
    return h * (1.0 + scale) + shift

def axial_rope(x):
    T = x.shape[1]
    t = jnp.arange(T)
    half = x.shape[-1] // 2
    inv_freq = ROPE_BASE ** (-jnp.arange(0, half, 2, dtype=F32) / half)

    def rot(xa, pos):
        ang = pos.astype(F32)[:, None] * inv_freq
        cos = jnp.cos(ang)[None, :, None, :]
        sin = jnp.sin(ang)[None, :, None, :]
        x1, x2 = jnp.split(xa, 2, axis=-1)
        return jnp.concatenate([x1 * cos - x2 * sin, x1 * sin + x2 * cos], axis=-1)

    return jnp.concatenate([rot(x[..., :half], t // GRID_W), rot(x[..., half:], t % GRID_W)], axis=-1)

def dw_conv(x, w):
    return lax.conv_general_dilated(
        x, w[:, None, :].astype(x.dtype), window_strides=(1,),
        padding=[(CONV_K // 2, CONV_K // 2)],
        dimension_numbers=("NWC", "WIO", "NWC"), feature_group_count=x.shape[-1])

def dense_context_attention(q, k, v):
    B, S, H, d = q.shape
    qb = q.reshape(B, S // CTX_QBLK, CTX_QBLK, H, d).transpose(1, 0, 2, 3, 4)

    def one_block(qblk):
        s = jnp.einsum("bqhd,bshd->bhqs", qblk, k).astype(F32)
        p = jax.nn.softmax(s, axis=-1).astype(v.dtype)
        return jnp.einsum("bhqs,bshd->bqhd", p, v)

    o = lax.map(one_block, qb)
    return o.transpose(1, 0, 2, 3, 4).reshape(B, S, H, d)

def neighbourhood_attention(q, k, v, k_ctx, v_ctx, rpb):
    B, T, H, d = q.shape
    rows = T // GRID_W
    kh = min(NA_KH, rows)
    ncb = GRID_W // NA_QCB
    r = np.arange(rows)
    row_idx = np.clip(r - kh // 2, 0, rows - kh)[:, None] + np.arange(kh)
    qcol = np.arange(GRID_W).reshape(ncb, NA_QCB)
    win_start = np.clip(qcol - NA_KW // 2, 0, GRID_W - NA_KW)
    kcol = np.clip(np.arange(ncb) * NA_QCB - NA_KW // 2, 0, GRID_W - NA_KCB)[:, None] + np.arange(NA_KCB)
    valid = (kcol[:, None, :] >= win_start[:, :, None]) & (kcol[:, None, :] < win_start[:, :, None] + NA_KW)
    dr = row_idx - r[:, None] + NA_KH - 1
    dc = np.clip(kcol[:, None, :] - qcol[:, :, None] + NA_KW - 1, 0, 2 * NA_KW - 2)
    bias = rpb[:, dr[:, None, None, :, None], dc[None, :, :, None, :]].astype(F32)
    bias = jnp.where(valid[None, None, :, :, None, :], bias, -jnp.inf)
    kg = k.reshape(B, rows, GRID_W, H, d)[:, row_idx][:, :, :, kcol]
    vg = v.reshape(B, rows, GRID_W, H, d)[:, row_idx][:, :, :, kcol]
    qb = q.reshape(B, rows, ncb, NA_QCB, H, d)
    s_loc = jnp.einsum("brjqhd,brijkhd->bhrjqik", qb, kg).astype(F32) + bias
    s_loc = s_loc.reshape(B, H, rows, ncb, NA_QCB, kh * NA_KCB)
    s_ctx = jnp.einsum("brjqhd,bshd->bhrjqs", qb, k_ctx).astype(F32)
    p = jax.nn.softmax(jnp.concatenate([s_loc, s_ctx], axis=-1), axis=-1).astype(v.dtype)
    p_loc = p[..., :kh * NA_KCB].reshape(B, H, rows, ncb, NA_QCB, kh, NA_KCB)
    p_ctx = p[..., kh * NA_KCB:]
    o = jnp.einsum("bhrjqik,brijkhd->brjqhd", p_loc, vg) + jnp.einsum("bhrjqs,bshd->brjqhd", p_ctx, v_ctx)
    return o.reshape(B, T, H, d)

def gated_delta_chunked(q, k, v, g, beta, s0):
    B, T, H, DK = q.shape
    n = T // GDN_CHUNK

    def blocks(a):
        a = a.reshape(B, n, GDN_CHUNK, H, *a.shape[3:])
        return jnp.moveaxis(a, 3, 1)

    q, k, v, g, beta = blocks(q), blocks(k), blocks(v), blocks(g), blocks(beta)
    gc = jnp.cumsum(g, axis=-1)
    i = np.arange(GDN_CHUNK)
    incl = i[:, None] >= i[None, :]
    strict = i[:, None] > i[None, :]
    decay = jnp.exp(jnp.where(incl, gc[..., :, None] - gc[..., None, :], -jnp.inf))
    kb = k * beta[..., None]
    a_mat = jnp.where(strict, jnp.einsum("bhnid,bhnjd->bhnij", kb, k) * decay, 0.0)
    eye = jnp.eye(GDN_CHUNK, dtype=F32)
    t_inv = lax.linalg.triangular_solve(eye + a_mat, jnp.broadcast_to(eye, a_mat.shape),
                                        left_side=True, lower=True, unit_diagonal=True)
    u = t_inv @ (v * beta[..., None])
    w = t_inv @ (kb * jnp.exp(gc)[..., None])
    qk = jnp.where(incl, jnp.einsum("bhnid,bhnjd->bhnij", q, k) * decay, 0.0)
    q_dec = q * jnp.exp(gc)[..., None]
    k_dec = k * jnp.exp(gc[..., -1:] - gc)[..., None]
    g_last = jnp.exp(gc[..., -1])
    xs = (jnp.moveaxis(u, 2, 0), jnp.moveaxis(w, 2, 0), jnp.moveaxis(qk, 2, 0),
          jnp.moveaxis(q_dec, 2, 0), jnp.moveaxis(k_dec, 2, 0), jnp.moveaxis(g_last, 2, 0))

    def step(s, inp):
        u_n, w_n, qk_n, qd_n, kd_n, gl_n = inp
        v_new = u_n - w_n @ s
        o_n = qd_n @ s + qk_n @ v_new
        s = s * gl_n[..., None, None] + jnp.einsum("bhck,bhcv->bhkv", kd_n, v_new)
        return s, o_n

    s_fin, o = lax.scan(step, s0, xs)
    o = o.transpose(1, 0, 3, 2, 4).reshape(B, T, H, v.shape[-1])
    return o, s_fin

def gdn_inputs(zqkv, zb, za, lw, axial):
    B, T, _ = zqkv.shape
    qkv = jax.nn.silu(dw_conv(zqkv, lw["gdn_conv_w"])).astype(F32)
    q, k, v = jnp.split(qkv, 3, axis=-1)
    q = l2_normalize(q.reshape(B, T, GDN_HEADS, GDN_DK))
    k = l2_normalize(k.reshape(B, T, GDN_HEADS, GDN_DK))
    v = v.reshape(B, T, GDN_HEADS, GDN_DV)
    if axial:
        q, k = axial_rope(q), axial_rope(k)
    q = q * GDN_DK ** -0.5
    beta = jax.nn.sigmoid(zb.astype(F32)).reshape(B, T, 2, GDN_HEADS)
    g = -jnp.exp(lw["gdn_a_log"].astype(F32)) * jax.nn.softplus(
        za.astype(F32).reshape(B, T, 2, GDN_HEADS) + lw["gdn_dt_bias"].astype(F32))
    return q, k, v, g, beta

def gdn_bidirectional(q, k, v, g, beta, s0):
    o_f, s_f = gated_delta_chunked(q, k, v, g[:, :, 0], beta[:, :, 0], s0[:, 0])
    fl = lambda a: jnp.flip(a, axis=1)
    o_b, s_b = gated_delta_chunked(fl(q), fl(k), fl(v), fl(g[:, :, 1]), fl(beta[:, :, 1]), s0[:, 1])
    return o_f + fl(o_b), jnp.stack([s_f, s_b], axis=1)

def gdn_output(o, zg, norm_g, dtype):
    B, T = o.shape[:2]
    o = rms_norm(o, norm_g) * jax.nn.silu(zg.astype(F32).reshape(B, T, GDN_HEADS, GDN_DV))
    return o.reshape(B, T, GDN_W).astype(dtype)

def na_heads(zq, zk, zv, lw):
    B, T, _ = zq.shape
    q = rms_norm(zq.reshape(B, T, NA_HEADS, NA_HD), lw["na_qn_g"]) * NA_HD ** -0.5
    k = rms_norm(zk.reshape(B, T, NA_HEADS, NA_HD), lw["na_kn_g"])
    v = zv.reshape(B, T, NA_HEADS, NA_HD)
    return q, k, v

def hier_moe(h, lw):
    B, T, D = h.shape
    t = h.reshape(-1, D)
    gp = jax.nn.softmax((t @ lw["moe_w_rg"] + lw["moe_b_rg"]).astype(F32), axis=-1)
    g_w, g_idx = lax.top_k(gp, 1)
    el = (t @ lw["moe_w_re"] + lw["moe_b_re"]).astype(F32).reshape(-1, N_GROUPS, EXP_PER_GROUP)
    el_sel = jnp.take_along_axis(el, g_idx[:, :, None], axis=1)[:, 0]
    ep = jax.nn.softmax(el_sel, axis=-1)
    e_w, e_idx = lax.top_k(ep, TOP_K)
    e_w = e_w / jnp.sum(e_w, axis=-1, keepdims=True)
    within = jnp.sum(jax.nn.one_hot(e_idx, EXP_PER_GROUP, dtype=F32) * e_w[..., None], axis=1)
    gate = jax.nn.one_hot(g_idx[:, 0], N_GROUPS, dtype=F32)[:, :, None] * (g_w[:, :, None] * within[:, None, :])
    gate = gate.reshape(-1, N_EXPERTS).astype(h.dtype)
    a = jnp.einsum("nd,edf->nef", t, lw["moe_w1"])
    b = jnp.einsum("nd,edf->nef", t, lw["moe_w3"])
    y = jnp.einsum("nef,efd->nd", jax.nn.silu(a) * b * gate[..., None], lw["moe_w2"])
    return y.reshape(B, T, D)

def context_layer(x, c_ctx, lw):
    B, S, _ = x.shape
    sh1, sc1, g1, sh2, sc2, g2 = modulation(c_ctx, lw)
    h = modulate(rms_norm(x, lw["norm1_g"]), sh1, sc1)
    zq, zk, zv, zqkv, zg, zb, za = jnp.split(h @ lw["w_in"], SPLITS, axis=-1)
    q, k, v = na_heads(zq, zk, zv, lw)
    o_na = dense_context_attention(q, k, v)
    gq, gk, gv, gg, gbeta = gdn_inputs(zqkv, zb, za, lw, axial=False)
    s0 = jnp.zeros((B, 2, GDN_HEADS, GDN_DK, GDN_DV), F32)
    o_g, s_fin = gdn_bidirectional(gq, gk, gv, gg, gbeta, s0)
    o_mix = jnp.concatenate([o_na.reshape(B, S, NA_W), gdn_output(o_g, zg, lw["gdn_norm_g"], x.dtype)], axis=-1)
    x = x + g1 * (o_mix @ lw["w_out"])
    x = x + g2 * hier_moe(modulate(rms_norm(x, lw["norm2_g"]), sh2, sc2), lw)
    return x, k, v, s_fin

def latent_layer(x, c, k_ctx, v_ctx, s_ctx, lw):
    B, T, _ = x.shape
    sh1, sc1, g1, sh2, sc2, g2 = modulation(c, lw)
    h = modulate(rms_norm(x, lw["norm1_g"]), sh1, sc1)
    zq, zk, zv, zqkv, zg, zb, za = jnp.split(h @ lw["w_in"], SPLITS, axis=-1)
    q, k, v = na_heads(zq, zk, zv, lw)
    o_na = neighbourhood_attention(q, k, v, k_ctx.astype(k.dtype), v_ctx.astype(v.dtype), lw["na_rpb"])
    gq, gk, gv, gg, gbeta = gdn_inputs(zqkv, zb, za, lw, axial=True)
    o_g, _ = gdn_bidirectional(gq, gk, gv, gg, gbeta, s_ctx.astype(F32))
    o_mix = jnp.concatenate([o_na.reshape(B, T, NA_W), gdn_output(o_g, zg, lw["gdn_norm_g"], x.dtype)], axis=-1)
    x = x + g1 * (o_mix @ lw["w_out"])
    x = x + g2 * hier_moe(modulate(rms_norm(x, lw["norm2_g"]), sh2, sc2), lw)
    return x

def setup_inputs(seed: int = 0) -> dict:
    key = jax.random.key(seed)
    ks = iter(jax.random.split(key, 32))

    def nrm(shape, scale):
        return scale * jax.random.normal(next(ks), shape, F32)

    def gain(shape):
        return 1.0 + nrm(shape, 0.05)

    a_log = jnp.log(jax.random.uniform(next(ks), (DEPTH, 2, GDN_HEADS), F32, minval=1.0, maxval=16.0))
    dt = jnp.exp(jax.random.uniform(next(ks), (DEPTH, 2, GDN_HEADS), F32,
                                    minval=math.log(1e-3), maxval=math.log(1e-1)))
    dt_bias = dt + jnp.log(-jnp.expm1(-dt))
    return {
        "x_prompt": nrm((BATCH, SEQ, D_MODEL), 1.0),
        "x_sample": nrm((DEC_BATCH, DEC_SEQ, D_MODEL), 1.0),
        "c": nrm((DEC_BATCH, D_MODEL), 1.0),
        "cache_k": nrm((DEC_BATCH, DEPTH, PAST_LEN, NA_HEADS, NA_HD), 1.0),
        "cache_v": nrm((DEC_BATCH, DEPTH, PAST_LEN, NA_HEADS, NA_HD), 1.0),
        "state_ssm": nrm((DEC_BATCH, DEPTH, 2, GDN_HEADS, GDN_DK, GDN_DV), GDN_DK ** -0.5),
        "c_ctx": nrm((D_MODEL,), 1.0),
        "ada_w": nrm((DEPTH, D_MODEL, 6 * D_MODEL), 0.5 * D_MODEL ** -0.5),
        "ada_b": nrm((DEPTH, 6 * D_MODEL), 0.02),
        "norm1_g": gain((DEPTH, D_MODEL)),
        "norm2_g": gain((DEPTH, D_MODEL)),
        "w_in": nrm((DEPTH, D_MODEL, N_IN), D_MODEL ** -0.5),
        "w_out": nrm((DEPTH, MIX_W, D_MODEL), MIX_W ** -0.5),
        "na_qn_g": gain((DEPTH, NA_HD)),
        "na_kn_g": gain((DEPTH, NA_HD)),
        "na_rpb": nrm((DEPTH, NA_HEADS, 2 * NA_KH - 1, 2 * NA_KW - 1), 0.1),
        "gdn_conv_w": nrm((DEPTH, CONV_K, 3 * GDN_W), CONV_K ** -0.5),
        "gdn_a_log": a_log,
        "gdn_dt_bias": dt_bias,
        "gdn_norm_g": gain((DEPTH, GDN_DV)),
        "moe_w_rg": nrm((DEPTH, D_MODEL, N_GROUPS), D_MODEL ** -0.5),
        "moe_b_rg": nrm((DEPTH, N_GROUPS), 0.01),
        "moe_w_re": nrm((DEPTH, D_MODEL, N_EXPERTS), D_MODEL ** -0.5),
        "moe_b_re": nrm((DEPTH, N_EXPERTS), 0.01),
        "moe_w1": nrm((DEPTH, N_EXPERTS, D_MODEL, EXPERT_FF), D_MODEL ** -0.5),
        "moe_w3": nrm((DEPTH, N_EXPERTS, D_MODEL, EXPERT_FF), D_MODEL ** -0.5),
        "moe_w2": nrm((DEPTH, N_EXPERTS, EXPERT_FF, D_MODEL), EXPERT_FF ** -0.5),
    }

def reference(x_prompt, x_sample, c, cache_k, cache_v, state_ssm, c_ctx, ada_w, ada_b, norm1_g, norm2_g,
              w_in, w_out, na_qn_g, na_kn_g, na_rpb, gdn_conv_w, gdn_a_log, gdn_dt_bias, gdn_norm_g,
              moe_w_rg, moe_b_rg, moe_w_re, moe_b_re, moe_w1, moe_w3, moe_w2):
    xp = x_prompt
    xs = x_sample
    ks, vs, ss = [], [], []
    for l in range(DEPTH):
        lw = {
            "ada_w": ada_w[l], "ada_b": ada_b[l], "norm1_g": norm1_g[l], "norm2_g": norm2_g[l],
            "w_in": w_in[l], "w_out": w_out[l], "na_qn_g": na_qn_g[l], "na_kn_g": na_kn_g[l],
            "na_rpb": na_rpb[l], "gdn_conv_w": gdn_conv_w[l], "gdn_a_log": gdn_a_log[l],
            "gdn_dt_bias": gdn_dt_bias[l], "gdn_norm_g": gdn_norm_g[l],
            "moe_w_rg": moe_w_rg[l], "moe_b_rg": moe_b_rg[l], "moe_w_re": moe_w_re[l], "moe_b_re": moe_b_re[l],
            "moe_w1": moe_w1[l], "moe_w3": moe_w3[l], "moe_w2": moe_w2[l],
        }
        xp, k_l, v_l, s_l = context_layer(xp, c_ctx, lw)
        ks.append(k_l)
        vs.append(v_l)
        ss.append(s_l)
        xs = latent_layer(xs, c, cache_k[:, l], cache_v[:, l], state_ssm[:, l], lw)
    y_prompt = xp
    y_sample = xs
    new_cache_k = jnp.stack(ks, axis=1)
    new_cache_v = jnp.stack(vs, axis=1)
    new_state_ssm = jnp.stack(ss, axis=1)
    return (y_prompt, y_sample, new_cache_k, new_cache_v, new_state_ssm)


_drawn_inputs = setup_inputs


def setup_inputs(seed=0):
    import zlib

    import numpy as np

    out = dict(_drawn_inputs(seed))
    spreads = {}
    factors = {'na_qn_g': 8.0,
     'na_rpb': 8.0,
     'gdn_norm_g': 4.275,
     'moe_b_rg': 37.759,
     'moe_b_re': 17.894,
     'norm2_g': 2.996}
    for name, (base, spread) in spreads.items():
        noise = np.random.default_rng([zlib.crc32(name.encode()), seed]).standard_normal(out[name].shape)
        drawn = base * np.exp(spread * noise) if base else spread * noise
        out[name] = jnp.asarray(drawn.astype(out[name].dtype))
    for name, factor in factors.items():
        out[name] = (out[name] * factor).astype(out[name].dtype)
    return out
```

```python
from contextlib import ExitStack

import concourse.bass as bass
import numpy as np
from concourse import mybir

ALU = mybir.AluOpType
ACT = mybir.ActivationFunctionType
F32 = mybir.dt.float32
BF16 = mybir.dt.bfloat16
I32 = mybir.dt.int32
U32 = mybir.dt.uint32
AX = mybir.AxisListType.X

P = 128
D = 1024
KC = D // P
CTX, LAT, PAST = 128, 256, 128
TOK = CTX + LAT
TILES = TOK // P
STREAM = [0, 1, 1]
DEPTH = 2
HEADS, HD = 8, 64
GRID_W, ROWS, NA_KW = 64, LAT // 64, 16
RPB_H, RPB_W = 15, 31
GH, GD = 4, 128
CONV = 5
N_IN = 3600
BA = 4 * GH
EXPERTS, GROUPS, PER = 16, 4, 4
FF = 512
EPS = 1e-6
BIG = 1.0e30
SLAB = 4096
N_ADA, N_WIN, N_OUT, N_MOE = 12, 7, 2, 3 * EXPERTS
EARLY = 4
PRE_SLOTS = 5
MOE_SLOTS = [1, 2, 3, 5, 4, 0]
POINTS = 24 + 3 * 12
NORM_AT = [7, 12, 17]
CHUNKS = [(0, 0), (1, 2), (2, 1)]
OUTS = [[0], [], [1, 2]]
N_SMALL = 3 * DEPTH + 7
N_SCRAP = 920
LEVELS = 7


def constants():
    t = np.arange(P)
    parts = {
        "ident": np.eye(P),
        "ones": np.ones((P, P)),
        "le": t[:, None] <= t[None, :],
        "ge": t[:, None] >= t[None, :],
        "gt": t[:, None] > t[None, :],
        "lt": t[:, None] < t[None, :],
    }
    levels = np.zeros((P, 2, LEVELS, P))
    for level in range(LEVELS):
        half = 1 << level
        block, upper = t // (2 * half), (t // half) % 2
        same = block[:, None] == block[None, :]
        levels[:, 0, level] = same & (upper[:, None] == 0) & (upper[None, :] == 1)
        levels[:, 1, level] = same & (upper[:, None] == 1) & (upper[None, :] == 0)
    parts["levels"] = levels
    half = GD // 2
    freq = (10000.0 ** (-np.arange(0, half, 2, dtype=np.float32) / np.float32(half))).astype(np.float32)
    tok = np.arange(LAT)
    cos, sin = np.zeros((P, 2, 2, 32), np.float32), np.zeros((P, 2, 2, 32), np.float32)
    for tile in range(2):
        for axis, pos in enumerate((tok // GRID_W, tok % GRID_W)):
            ang = pos[tile * P:(tile + 1) * P].astype(np.float32)[:, None] * freq
            cos[:, tile, axis], sin[:, tile, axis] = np.cos(ang), np.sin(ang)
    parts["cos"], parts["sin"] = cos, sin
    col = GRID_W - 1 - t % GRID_W
    parts["flip"] = (t[:, None] // GRID_W == t[None] // GRID_W) & (col[:, None] == t[None] % GRID_W)
    start = np.clip(col - NA_KW // 2, 0, GRID_W - NA_KW)
    kcol = np.arange(GRID_W)
    inside = (kcol[None] >= start[:, None]) & (kcol[None] < start[:, None] + NA_KW)
    parts["window"] = np.broadcast_to(np.where(inside, 0.0, -BIG)[:, None], (P, ROWS, GRID_W))
    parts["first"] = np.broadcast_to(4.0 - np.arange(4), (P, 4))
    parts["row0"] = np.broadcast_to(np.arange(EXPERTS) * 1.0, (P, EXPERTS))
    parts["slot"] = np.broadcast_to(t.astype(np.float64), (P, P))
    parts["tokid"] = np.stack([np.stack([t, np.full(P, tile)], 1) for tile in range(TILES)], 1)
    parts["eps"] = np.full((P, 1), EPS)
    at, where, cols = 0, {}, []
    for name, a in parts.items():
        a = np.asarray(a, np.float32)
        where[name] = (at, a.shape[1:])
        cols.append(a.reshape(P, -1))
        at += cols[-1].shape[1]
    return where, np.ascontiguousarray(np.concatenate(cols, 1))


def pre_slabs():
    out = []
    for l in range(DEPTH):
        ada = [("ada", l, i) for i in range(EARLY, N_ADA)]
        if l + 1 < DEPTH:
            ada += [("ada", l + 1, i) for i in range(EARLY)]
        first = [("ada", 0, i) for i in range(EARLY)] if l == 0 else []
        out.append(first + [("win", l, j) for j in range(N_WIN)] + ada + [("wout", l, j) for j in range(N_OUT)])
    return out


def mixing_plan(slabs):
    products, rows_at, cols_at = [], [[] for _ in range(POINTS)], [[] for _ in range(POINTS)]
    todo = [(s, k) for s in slabs for k in range(KC)]
    late = (len(todo) - 24) / (POINTS - 24 - 3)
    due, made = 0.0, 0
    for point in range(POINTS):
        due += 1.0 if point < 24 else late
        now = []
        while todo and made < due - 1e-6:
            now.append(todo.pop(0))
            made += 1
            if now[-1][1] == KC - 1:
                break
        products.append(now)
        for s, k in now:
            if k == KC - 1:
                rows_at[point + 1].append(s)
                cols_at[point + 2].append(s)
    assert not todo
    return list(zip(products, rows_at, cols_at))


class Counts:

    def __init__(self):
        self.seen = {}

    def __call__(self, sem, more=1):
        self.seen[sem.name] = self.seen.get(sem.name, 0) + more
        return self.seen[sem.name]


def over(ap, n):
    return ap.unsqueeze(2).broadcast_to([ap.shape[0], ap.shape[1], n])


def heads(ap, n):
    return ap.unsqueeze(1).broadcast_to([ap.shape[0], n, ap.shape[1]])


def flat(a):
    return a.rearrange("p h n -> p (h n)")


def program(nc, x_prompt, x_sample, c, cache_k, cache_v, state_ssm, c_ctx, ada_w, ada_b, norm1_g,
            norm2_g, w_in, w_out, na_qn_g, na_kn_g, na_rpb, gdn_conv_w, gdn_a_log, gdn_dt_bias,
            gdn_norm_g, moe_w_rg, moe_b_rg, moe_w_re, moe_b_re, moe_w1, moe_w3, moe_w2, tables,
            y_prompt, y_sample, new_k, new_v, new_state, where, debug=None, CAP=P):
    OVER = (TOK + CAP - 1) // CAP - 1
    ctx = ExitStack()
    with ctx:
        def sb(name, shape, dt=F32):
            return ctx.enter_context(nc.sbuf_tensor(name, shape, dt))

        def sem(name):
            return ctx.enter_context(nc.semaphore(name))

        bank = [ctx.enter_context(nc.psum_tensor(f"bank{i}", [P, 512], F32)) for i in range(8)]
        tok_dram = nc.dram_tensor("tok_dram", [TOK, D], F32, kind="Internal").ap()
        expert_dram = nc.dram_tensor("expert_dram", [(1 + OVER) * EXPERTS * CAP, D], F32, kind="Internal").ap()

        const = sb("const", list(tables.shape))
        ring = sb("ring", [P, PRE_SLOTS, SLAB])
        x = sb("x", [P, TILES, D])
        hT = sb("hT", [P, KC, TOK])
        cols = sb("cols", [P, 3, P])
        silu_c = sb("silu_c", [P, 16])
        mods = sb("mod", [P, DEPTH, 48, 2])
        mrow = sb("mrow", [2, 2, 512])
        w_ba = sb("w_ba", [P, DEPTH, KC, BA])
        w_rt = sb("w_rt", [P, DEPTH, KC, GROUPS + EXPERTS])
        b_rt = sb("b_rt", [P, DEPTH, GROUPS + EXPERTS])
        head_g = sb("head_g", [P, DEPTH, 2, HD])
        gdn_g = sb("gdn_g", [P, DEPTH, GD])
        gate_c = sb("gate_c", [P, DEPTH, 2, 8])
        small = sb("small", [P, N_SCRAP])
        idx = sb("idx", [P, EXPERTS], U32)
        idx_now = sb("idx_now", [P, 2], U32)
        idx_row = sb("idx_row", [P, TILES, 2], U32)
        most = sb("most", [1, 1], I32)
        tokid_b = sb("tokid_b", [P, TILES, 2], BF16)
        arena = sb("arena", [P, 19456])

        def tab(name):
            at, shape = where[name]
            size = int(np.prod(shape))
            flat = const[:, at:at + size]
            if len(shape) == 1:
                return flat
            names = "abcd"[:len(shape)]
            return flat.rearrange(f"p ({' '.join(names)}) -> p {' '.join(names)}",
                                  **{k: int(v) for k, v in zip(names, shape)})

        at_now = [0]

        def take(n, reset=None):
            if reset is not None:
                at_now[0] = reset
            at_now[0] += n
            assert at_now[0] <= 19456, at_now[0]
            return arena[:, at_now[0] - n:at_now[0]]

        ident, ones = tab("ident"), tab("ones")
        rows = take(3 * P, 0).rearrange("p (r n) -> p r n", r=3)
        gq = take(3 * 1536, 0).rearrange("p (t s h d) -> p t s h d", t=TILES, s=3, h=GH)
        zg = take(3 * 512).rearrange("p (t n) -> p t n", t=TILES)
        z = take(3 * 512, 6144).rearrange("p (t n) -> p t n", t=TILES)
        v_sb = take(3 * 512).rearrange("p (t n) -> p t n", t=TILES)
        v_past = take(512)
        k_past = take(512)
        qT = take(4 * TOK).rearrange("p (h n) -> p h n", h=4)
        kT = take(4 * 512).rearrange("p (h n) -> p h n", h=4)
        bias = take(2 * 1024).rearrange("p (b h n) -> p b h n", b=2, h=4)
        z_k = take(3 * 512, at_now[0] - 2048).rearrange("p (t n) -> p t n", t=TILES)
        at_now[0] += 512
        scratch = at_now[0]
        sq = take(1024).rearrange("p (b n) -> p b n", b=2)
        take(768)
        p_sb = take(768).rearrange("p (b n) -> p b n", b=2)
        pT = take(768).rearrange("p (b n) -> p b n", b=2)
        o_na = z[:, 0, :]
        SQ0 = scratch
        sq8 = take(1024, scratch).rearrange("p (h n) -> p h n", h=8)
        turn = take(1536, scratch).rearrange("p (b h a n) -> p b h a n", b=3, h=8, a=2)
        xn = take(2048, scratch).rearrange("p (b n) -> p b n", b=2)
        CW = 2 + CTX + 2 + 2 + LAT + 2
        CO = CW - 4
        conv_in = take(2 * CW, scratch + 1024).rearrange("p (b n) -> p b n", b=2)
        conv_acc = take(2 * CO).rearrange("p (b n) -> p b n", b=2)
        take(0, 6144)
        gb = [[take(512).rearrange("p (h n) -> p h n", h=GH) for _ in range(11)] for _ in range(2)]
        state = [take(512).rearrange("p (h n) -> p h n", h=GH) for _ in range(2)]
        o_acc = take(1024).rearrange("p (t n) -> p t n", t=2)
        slot5 = take(SLAB, 0)
        x_e = take(2048).rearrange("p (b n) -> p b n", b=2)
        xT_e = take(2048).rearrange("p (b k n) -> p b k n", b=2, k=KC)
        silu_a = take(1024).rearrange("p (b n) -> p b n", b=2)
        h_e = take(1024).rearrange("p (b n) -> p b n", b=2)
        hT_e = take(1024).rearrange("p (b k n) -> p b k n", b=2, k=4)
        y_e = take(2048).rearrange("p (b n) -> p b n", b=2)
        xn2 = y_e
        sel = take(768).bitcast(BF16).rearrange("p (t e n) -> p t e n", t=TILES, e=4)
        gate_b = take(2048).rearrange("p (s n) -> p s n", s=2)
        tok_sb = take(3072).rearrange("p (t n) -> p t n", t=TILES)
        y_first = hT[:].rearrange("p k n -> p (k n)").rearrange("p (t n) -> p t n", t=TILES)
        y_second = take(3072, SLAB).rearrange("p (t n) -> p t n", t=TILES)

        at_small = [0]

        def sm(n):
            at_small[0] += n
            assert at_small[0] <= N_SCRAP
            return small[:, at_small[0] - n:at_small[0]]

        def smt(n):
            return sm(TILES * n).rearrange("p (t n) -> p t n", t=TILES)

        ss, rstd = sm(TILES), sm(TILES)
        hss = sm(16).rearrange("p (b n) -> p b n", b=2)
        hr = sm(16).rearrange("p (b n) -> p b n", b=2)
        ba, beta, decay, ga, gabs, ea = smt(16), smt(8), smt(8), smt(8), smt(8), sm(8)
        qss, qr = smt(8), smt(8)
        neg_max, row_sum = smt(8), smt(8)
        gsum, gexp = [sm(12) for _ in range(2)], [sm(12) for _ in range(2)]
        oss, orr = sm(4), sm(4)
        lg, r_exp = smt(20), smt(5)
        m_g, m_1, m_2, t3 = (sm(TILES) for _ in range(4))
        oh_g, oh1, oh2, el = (smt(4) for _ in range(4))
        t16 = smt(16)
        w_tok, rowf = smt(2), smt(2)
        choice = sm(96).rearrange("p (t c n) -> p t c n", t=TILES, c=2)
        chosen, place, shifted = smt(16), smt(16), smt(16)
        pair_f, t1 = sm(8), sm(1)

        consts_in, rows_in, weights_in, x_in = map(sem, ("consts_in", "rows_in", "weights_in", "x_in"))
        dve_step, act_step, pool_step = map(sem, ("dve_step", "act_step", "pool_step"))
        for_dve, dve_emptied = sem("for_dve"), sem("dve_emptied")
        ada_full, ada_taken = sem("ada_full"), sem("ada_taken")
        sq_ready, combine_a, combine_b, combine_c = map(sem, ("sq_ready", "combine_a", "combine_b", "combine_c"))
        for_act, act_emptied = sem("for_act"), sem("act_emptied")
        slab_in = [sem(f"slab_in{i}") for i in range(PRE_SLOTS)]
        moe_in = [sem(f"moe_in{i}") for i in range(6)]
        silu_c_ready = sem("silu_c_ready")
        ln_asked = sem("ln_asked")
        rs_ready = sem("rs_ready")
        xn_ready = sem("xn_ready")
        z_ready = sem("z_ready")
        zn_ready = sem("zn_ready")
        k_out_ready = sem("k_out_ready")
        past_in = sem("past_in")
        kv_stored = sem("kv_stored")
        conv_in_ready = sem("conv_in_ready")
        conv_ready = sem("conv_ready")
        silu_ready = sem("silu_ready")
        zg_in = sem("zg_in")
        gates_x = sem("gates_x")
        gates_e = sem("gates_e")
        gates_ready = sem("gates_ready")
        gq_normed = sem("gq_normed")
        bias_in = sem("bias_in")
        bias_ready = sem("bias_ready")
        s_ready = sem("s_ready")
        pT_ready = sem("pT_ready")
        pv_done = sem("pv_done")
        o_na_ready = sem("o_na_ready")
        decay_rhs = sem("decay_rhs")
        gsum_ready = sem("gsum_ready")
        gexp_ready = sem("gexp_ready")
        gdn_scaled = sem("gdn_scaled")
        lvl_ready = sem("lvl_ready")
        state_in = sem("state_in")
        state_out = sem("state_out")
        og_ready = sem("og_ready")
        x_ready = sem("x_ready")
        diag_ready = sem("diag_ready")
        tok_ready = sem("tok_ready")
        tok_stored = sem("tok_stored")
        routed = sem("routed")
        y_in = [sem(f"y_in{t}") for t in range(TILES)]
        c_exp, pads_ready, state_zero = sem("c_exp"), sem("pads_ready"), sem("state_zero")
        pool_scaled = sem("pool_scaled")
        router_x, router_e, counted = sem("router_x"), sem("router_e"), sem("counted")
        out_stored = sem("out_stored")

        def expert_sems(tag):
            names = ("step", "gathering", "sel", "list_full", "list_taken", "idx_copied", "transposed", "xT", "a_full", "b_full",
                     "silu", "h", "hTp", "hT", "y_full", "y")
            s = {k: sem(f"{tag}_{k}") for k in names}
            s["gathered"] = [sem(f"{tag}_gathered{b}") for b in range(2)]
            s["y_stored"] = [sem(f"{tag}_y_stored{b}") for b in range(2)]
            return s

        es = expert_sems("moe")
        spare = [expert_sems(f"over{l}") for l in range(DEPTH)]
        spare_in = [[sem(f"over{l}_in{i}") for i in range(6)] for l in range(DEPTH)]

        def slot(s):
            return ring[:, s, :] if s < PRE_SLOTS else slot5

        def wide(s):
            return slot(s).rearrange("p (k n) -> p k n", k=KC)

        PRE = pre_slabs()
        pre_slot, pre_turn, held = {}, {}, [0] * PRE_SLOTS
        for slabs in PRE:
            for i, name in enumerate(slabs):
                pre_slot[name] = (i - len(slabs) + 1) % PRE_SLOTS
                held[pre_slot[name]] += 1
                pre_turn[name] = held[pre_slot[name]]

        def arrived(eng, *name):
            eng.wait_ge(slab_in[pre_slot[name]], 16 * pre_turn[name])

        def store_debug(eng, name, ap):
            if debug and name in debug:
                eng.dma_start(debug[name], ap).then_inc(out_stored, 16)

        slab_job = {}
        job = {}
        block = ctx.enter_context(nc.Block())

        @block.tensor
        def _(pe):
            n = Counts()
            jobs = {"dve": 0, "act": 0, "ada": 0}

            def dve_bank(*name):
                b = jobs["dve"]
                jobs["dve"] += 1
                job[name] = b + 1
                if b >= 3:
                    pe.wait_ge(dve_emptied, b - 2)
                return bank[b % 3]

            def act_bank(*name):
                b = jobs["act"]
                jobs["act"] += 1
                job[name] = b + 1
                if b >= 3:
                    pe.wait_ge(act_emptied, b - 2)
                return bank[4 + b % 3]

            def mm(out, lhsT, rhs, start=True, stop=True):
                return nc.tensor.matmul(out, lhsT, rhs, start=start, stop=stop)

            def tr(out, src, rows_=P):
                return nc.tensor.transpose(out, src, ident[0:rows_, 0:rows_])

            def tr4(b, src):
                for q in range(4):
                    last = tr(b[:, q * P:(q + 1) * P], src[:, q * P:(q + 1) * P])
                return last

            pe.wait_ge(consts_in, 16)
            pe.wait_ge(rows_in, 96)
            b = dve_bank("cols")
            tr(b[:, 0:P], rows[:, 0, :])
            tr(b[:, P:P + 120], rows[0:120, 1, :], 120)
            tr(b[:, 256:272], rows[0:16, 2, :], 16).then_inc(for_dve, 1)
            pe.wait_ge(silu_c_ready, 1)

            def ada_product(slab, k):
                if k == 0:
                    arrived(pe, *slab)
                    if jobs["ada"]:
                        pe.wait_ge(ada_taken, jobs["ada"])
                last = mm(bank[3][0:2, :], silu_c[:, k:16:8], wide(pre_slot[slab])[:, k, :], k == 0, k == KC - 1)
                if k == KC - 1:
                    last.then_inc(ada_full, 1)
                    jobs["ada"] += 1
                    slab_job[slab] = ("ada", jobs["ada"])

            def ada_cols(slab):
                no = slab_job[slab][1]
                pe.wait_ge(ada_taken, no)
                b = dve_bank("mod_col", *slab)
                for q in range(4):
                    last = tr(b[:, 2 * q:2 * q + 2], mrow[:, (no - 1) % 2, q * P:(q + 1) * P], 2)
                last.then_inc(for_dve, 1)

            for i in range(EARLY):
                for k in range(KC):
                    ada_product(("ada", 0, i), k)
                if i:
                    ada_cols(("ada", 0, i - 1))
            ada_cols(("ada", 0, EARLY - 1))
            for l in range(DEPTH):
                plan = mixing_plan([name for name in PRE[l][EARLY if l == 0 else 0:] if name[0] == "ada"])

                def point(p):
                    products, _, cols_ = plan[p]
                    for slab in cols_:
                        ada_cols(slab)
                    for slab, k in products:
                        ada_product(slab, k)

                def transposed_norm(which):
                    for t in range(TILES):
                        pe.wait_ge(xn_ready, n(xn_ready))
                        for half in range(2):
                            b = dve_bank("norm", l, which, t, half)
                            tr4(b, (xn, xn2)[which - 1][:, t % 2, half * 512:(half + 1) * 512]).then_inc(for_dve, 1)
                    pe.wait_ge(dve_emptied, job["norm", l, which, TILES - 1, 1])

                transposed_norm(1)

                def token_major(i, t):
                    w = wide(pre_slot["win", l, i])
                    b = act_bank("win", l, i, t)
                    for k in range(KC):
                        last = mm(b[:], hT[:, k, t * P:(t + 1) * P], w[:, k, :], k == 0, k == KC - 1)
                    last.then_inc(for_act, 1)
                    slab_job["win", l, i] = ("act", jobs["act"])

                for i in range(3):
                    arrived(pe, "win", l, i)
                    for t in range(TILES):
                        token_major(i, t)
                        if i:
                            pe.wait_ge(zn_ready, n(zn_ready))
                            b = act_bank("qkT", l, i - 1, t)
                            tr4(b, (z, z_k)[i - 1][:, t, :]).then_inc(for_act, 1)
                pe.wait_ge(past_in, 32 * (l + 1))
                b = act_bank("past", l)
                tr4(b, k_past).then_inc(for_act, 1)

                def conv_cols(f):
                    pe.wait_ge(silu_ready, n(silu_ready))
                    b = act_bank("conv_back", l, f)
                    off = (0, CTX + 4, CTX + 4 + P)
                    for t in range(TILES):
                        last = tr(b[:, t * P:(t + 1) * P], conv_acc[:, f % 2, off[t]:off[t] + P])
                    last.then_inc(for_act, 1)

                for f in range(12):
                    slab = ("win", l, 3 + f // 4)
                    if f % 4 == 0:
                        arrived(pe, *slab)
                    w = wide(pre_slot[slab])
                    b = act_bank("conv", l, f)
                    for k in range(KC):
                        last = mm(b[:, 0:TOK], w[:, k, (f % 4) * P:(f % 4 + 1) * P], hT[:, k, :], k == 0, k == KC - 1)
                    last.then_inc(for_act, 1)
                    slab_job[slab] = ("act", jobs["act"])
                    if f:
                        conv_cols(f - 1)
                conv_cols(11)
                arrived(pe, "win", l, 6)
                for t in range(TILES):
                    token_major(6, t)
                pe.wait_ge(weights_in, 16 * N_SMALL)
                b = dve_bank("ba", l)
                for t in range(TILES):
                    for k in range(KC):
                        last = mm(b[:, t * BA:(t + 1) * BA], hT[:, k, t * P:(t + 1) * P], w_ba[:, l, k, :],
                                  k == 0, k == KC - 1)
                last.then_inc(for_dve, 1)

                units = [(t, h) for t in range(TILES) for h in range(HEADS)]

                def score(u):
                    t, h = units[u]
                    half = slice(64 * (h % 2), 64 * (h % 2) + 64)
                    keys = slice(0, P) if t == 0 else slice(P, 512)
                    b = act_bank("score", l, u)
                    last = mm(b[:, 0:keys.stop - keys.start], qT[half, h // 2, t * P:(t + 1) * P],
                              kT[half, h // 2, keys], True, t == 0)
                    if t:
                        pe.wait_ge(bias_ready, 4 * l + 2 * (t - 1) + h // 4 + 1)
                        last = mm(b[:, 0:LAT], tab("flip"), bias[:, h // 4, h % 4, :], False, True)
                    last.then_inc(for_act, 1)

                def probs_cols(u):
                    t, h = units[u]
                    pe.wait_ge(act_emptied, job["score", l, u])
                    b = act_bank("probs", l, u)
                    for q in range(1 if t == 0 else 3):
                        last = tr(b[:, q * P:(q + 1) * P], p_sb[:, u % 2, q * P:(q + 1) * P])
                    last.then_inc(for_act, 1)

                def weigh(u):
                    t, h = units[u]
                    pe.wait_ge(act_emptied, job["probs", l, u])
                    if h == 0 and (t or l):
                        pe.wait_ge(o_na_ready, 3 * l + t)
                    values = [v_sb[:, 0, :]] if t == 0 else [v_sb[:, 1, :], v_sb[:, 2, :], v_past]
                    for q, v in enumerate(values):
                        last = mm(bank[7][:, h * HD:(h + 1) * HD], pT[:, u % 2, q * P:(q + 1) * P],
                                  v[:, h * HD:(h + 1) * HD], q == 0, q == len(values) - 1)
                    last.then_inc(pv_done, 1)

                def mixed_cols(ready, src, *name):
                    pe.wait_ge(ready, n(ready))
                    tr4(act_bank(*name), src).then_inc(for_act, 1)

                pe.wait_ge(act_emptied, job["past", l])
                score(0)
                score(1)
                for u in range(len(units)):
                    probs_cols(u)
                    if u > 2 and u % 8 == 2:
                        mixed_cols(o_na_ready, o_na, "o_na", l, u // 8 - 1)
                    if u:
                        weigh(u - 1)
                    if u + 2 < len(units):
                        score(u + 2)
                    point(u)
                weigh(len(units) - 1)
                mixed_cols(o_na_ready, o_na, "o_na", l, 2)

                pe.wait_ge(gates_ready, l + 1)
                pe.wait_ge(gq_normed, 3 * l + 3)
                for step in range(3):
                    chunks = CHUNKS[step]
                    for d in range(2):
                        t = chunks[d]
                        b = dve_bank("gsum", l, step, d)
                        mm(b[:, 0:4], tab(("le", "ge")[d]), decay[:, t, 4 * d:4 * d + 4])
                        mm(b[:, 4:8], ones, decay[:, t, 4 * d:4 * d + 4]).then_inc(for_dve, 1)
                        pe.wait_ge(decay_rhs, n(decay_rhs))
                        b = act_bank("dt", l, step, d)
                        mm(b[:], tab(("gt", "lt")[d]), flat(gb[d][0])).then_inc(for_act, 1)
                    for d in range(2):
                        t = chunks[d]
                        pe.wait_ge(gdn_scaled, n(gdn_scaled))
                        for m, src in enumerate((gb[d][2], gq[:, t, 1], gq[:, t, 0], gb[d][4])):
                            b = act_bank("gT", l, step, d, m)
                            for h in range(GH):
                                last = tr(b[:, h * P:(h + 1) * P], src[:, h, :])
                            last.then_inc(for_act, 1)
                    for d in range(2):
                        pe.wait_ge(act_emptied, job["gT", l, step, d, 3])
                        for name, rhs in (("qk", gb[d][9]), ("kk", gb[d][8])):
                            b = dve_bank(name, l, step, d)
                            for h in range(GH):
                                last = mm(b[:, h * P:(h + 1) * P], gb[d][10][:, h, :], rhs[:, h, :])
                            last.then_inc(for_dve, 1)
                    for d in range(2):
                        pe.wait_ge(lvl_ready, n(lvl_ready))
                        b = dve_bank("t0", l, step, d)
                        for h in range(GH):
                            last = tr(b[:, h * P:(h + 1) * P], gb[d][0][:, h, :])
                        last.then_inc(for_dve, 1)
                    for level in range(1, LEVELS):
                        before = ("t0", l, step) if level == 1 else ("tu", l, step, level - 1)
                        for d in range(2):
                            pe.wait_ge(lvl_ready, n(lvl_ready))
                            pe.wait_ge(dve_emptied, job[(*before, d)])
                            b = act_bank("at", l, step, level, d)
                            for h in range(GH):
                                last = mm(b[:, h * P:(h + 1) * P], gb[d][0][:, h, :], gb[d][2][:, h, :])
                            last.then_inc(for_act, 1)
                        point(24 + 12 * step + 2 * (level - 1))
                        for d in range(2):
                            pe.wait_ge(act_emptied, job["at", l, step, level, d])
                            if level < LEVELS - 1:
                                b = dve_bank("tat", l, step, level, d)
                                for h in range(GH):
                                    last = mm(b[:, h * P:(h + 1) * P], gb[d][4][:, h, :], gb[d][1][:, h, :])
                                last.then_inc(for_dve, 1)
                            b = dve_bank("tu", l, step, level, d)
                            for h in range(GH):
                                last = mm(b[:, h * P:(h + 1) * P], gb[d][1][:, h, :], gb[d][4][:, h, :])
                            last.then_inc(for_dve, 1)
                        point(24 + 12 * step + 2 * (level - 1) + 1)
                    for d in range(2):
                        pe.wait_ge(dve_emptied, job["tu", l, step, LEVELS - 1, d])
                        b = act_bank("wT", l, step, d)
                        for h in range(GH):
                            last = mm(b[:, h * P:(h + 1) * P], gb[d][3][:, h, :], gb[d][4][:, h, :])
                        last.then_inc(for_act, 1)
                    for d in range(2):
                        pe.wait_ge(act_emptied, job["wT", l, step, d])
                        pe.wait_ge(pool_scaled, 6 * l + 2 * step + d + 1)
                        if step == 0:
                            pe.wait_ge(state_zero, 2 * l + d + 1)
                        elif step == 1:
                            pe.wait_ge(state_in, 32 * (l + 1))
                        else:
                            pe.wait_ge(dve_emptied, job["kv", l, 1, d])
                        b = dve_bank("vnew", l, step, d)
                        for h in range(GH):
                            mm(b[:, h * P:(h + 1) * P], gb[d][4][:, h, :], gb[d][7][:, h, :], True, False)
                            last = mm(b[:, h * P:(h + 1) * P], gb[d][8][:, h, :], state[d][:, h, :], False, True)
                        last.then_inc(for_dve, 1)
                    for d in range(2):
                        pe.wait_ge(dve_emptied, job["vnew", l, step, d])
                        b = dve_bank("o", l, step, d)
                        for h in range(GH):
                            mm(b[:, h * P:(h + 1) * P], gb[d][5][:, h, :], state[d][:, h, :], True, False)
                            last = mm(b[:, h * P:(h + 1) * P], gb[d][9][:, h, :], gb[d][0][:, h, :], False, True)
                        last.then_inc(for_dve, 1)
                        b = dve_bank("kv", l, step, d)
                        for h in range(GH):
                            last = mm(b[:, h * P:(h + 1) * P], gb[d][6][:, h, :], gb[d][0][:, h, :])
                        last.then_inc(for_dve, 1)
                    for t in OUTS[step]:
                        mixed_cols(og_ready, flat(gb[1][1]), "og", l, t)
                pe.wait_ge(act_emptied, job["og", l, 2])

                def gate_rows(which):
                    for s in range(2):
                        for half in range(2):
                            pe.wait_ge(diag_ready, n(diag_ready))
                            b = dve_bank("gate", l, which, s, half)
                            mm(b[:], ones, silu_a[:, half, :]).then_inc(for_dve, 1)

                gate_rows(1)
                for j in range(N_OUT):
                    arrived(pe, "wout", l, j)
                    w = wide(pre_slot["wout", l, j])
                    for t in range(TILES):
                        b = dve_bank("wout", l, j, t)
                        for k in range(KC):
                            last = mm(b[:], hT[:, k, t * P:(t + 1) * P], w[:, k, :], k == 0, k == KC - 1)
                        last.then_inc(for_dve, 1)
                    slab_job["wout", l, j] = ("dve", jobs["dve"])
                transposed_norm(2)
                b = dve_bank("router", l)
                for t in range(TILES):
                    for k in range(KC):
                        last = mm(b[:, t * 20:(t + 1) * 20], hT[:, k, t * P:(t + 1) * P], w_rt[:, l, k, :],
                                  k == 0, k == KC - 1)
                last.then_inc(for_dve, 1)
                for t in range(TILES):
                    for half in range(2):
                        b = act_bank("tok", l, t, half)
                        for q in range(4):
                            last = tr(b[:, q * P:(q + 1) * P], hT[:, 4 * half + q, t * P:(t + 1) * P])
                        last.then_inc(for_act, 1)
                gate_rows(2)
                pe.wait_ge(routed, l + 1)
                b = dve_bank("place", l)
                for t in range(TILES):
                    for s in range(t + 1):
                        mm(b[:, t * 16:(t + 1) * 16], tab("lt") if s == t else ones, chosen[:, s, :],
                           s == 0, s == t)
                for s in range(TILES):
                    last = mm(b[:, 48:64], ones, chosen[:, s, :], s == 0, s == TILES - 1)
                last.then_inc(for_dve, 1)

                def run_experts(s, slab_sems, first):
                    def tokens(e, j, pair):
                        pe.wait_ge(s["gathered"][j], 16 * (pair + 1))
                        for half in range(2):
                            tr4(bank[half], x_e[:, j, half * 512:(half + 1) * 512]).then_inc(s["transposed"], 1)

                    def up(e, j, pair):
                        w1, w3 = (wide(MOE_SLOTS[3 * j + m]) for m in range(2))
                        pe.wait_ge(s["xT"], e * 2 + 2)
                        pe.wait_ge(slab_sems[3 * j], 16 * (pair + 1))
                        for k in range(KC):
                            last = mm(bank[2 + j][:], xT_e[:, j, k, :], w1[:, k, :], k == 0, k == KC - 1)
                        last.then_inc(s["a_full"], 1)
                        pe.wait_ge(slab_sems[3 * j + 1], 16 * (pair + 1))
                        for k in range(KC):
                            last = mm(bank[4 + j][:], xT_e[:, j, k, :], w3[:, k, :], k == 0, k == KC - 1)
                        last.then_inc(s["b_full"], 1)

                    def down(e, j, pair, first_ever=False):
                        w2 = slot(MOE_SLOTS[3 * j + 2]).rearrange("p (k n) -> p k n", k=4)
                        pe.wait_ge(s["h"], e + 1)
                        tr4(bank[0], h_e[:, j, :]).then_inc(s["hTp"], 1)
                        pe.wait_ge(s["hT"], e + 1)
                        pe.wait_ge(slab_sems[3 * j + 2], 16 * (pair + 1))
                        for half in range(2):
                            if not first_ever:
                                pe.wait_ge(s["y"], e * 2 + half - 1)
                            for k in range(4):
                                last = mm(bank[6 + half][:], hT_e[:, j, k, :], w2[:, k, half * 512:(half + 1) * 512],
                                          k == 0, k == 3)
                            last.then_inc(s["y_full"], 1)

                    for group in range(4):
                        g = first // 4 + group
                        pe.wait_ge(s["sel"], g + 1)
                        if g >= 2:
                            pe.wait_ge(s["list_taken"], g - 1)
                        for e in range(4):
                            for t in range(TILES):
                                last = mm(bank[6 + group % 2][:, 2 * e:2 * e + 2], sel[:, t, e, :], tokid_b[:, t, :],
                                          t == 0, t == TILES - 1)
                        last.then_inc(s["list_full"], 1)
                    pe.wait_ge(s["list_taken"], first // 4 + 4)
                    pair = first // 2
                    tokens(first, 0, pair)
                    up(first, 0, pair)
                    tokens(first + 1, 1, pair)
                    up(first + 1, 1, pair)
                    down(first, 0, pair, first == 0)
                    with pe.Fori(1, EXPERTS // 2) as i:
                        e = i * 2 + first
                        tokens(e, 0, i + pair)
                        up(e, 0, i + pair)
                        down(e - 1, 1, i + (pair - 1))
                        tokens(e + 1, 1, i + pair)
                        up(e + 1, 1, i + pair)
                        down(e, 0, i + pair)
                    down(first + EXPERTS - 1, 1, pair + EXPERTS // 2 - 1)
                    pe.wait_ge(s["y"], 2 * (first + EXPERTS))

                pe.wait_ge(dve_emptied, jobs["dve"])
                pe.wait_ge(act_emptied, jobs["act"])
                run_experts(es, moe_in, l * EXPERTS)
                pe.wait_ge(counted, l + 1)
                top = pe.value_load(most[0:1, 0:1])
                with pe.If(top > CAP):
                    for again in range(OVER):
                        run_experts(spare[l], spare_in[l], again * EXPERTS)

        @block.sync
        def _(sp):
            n = Counts()
            sp.dma_start(rows[0:96, 0, :], ada_b.rearrange("l (j p) -> (l j) p", p=P)).then_inc(rows_in, 16)
            sp.dma_start(rows[96:112, 0, :], norm1_g.rearrange("l (k p) -> (l k) p", p=P)).then_inc(rows_in, 16)
            sp.dma_start(rows[112:128, 0, :], norm2_g.rearrange("l (k p) -> (l k) p", p=P)).then_inc(rows_in, 16)
            sp.dma_start(rows[0:120, 1, :], gdn_conv_w.rearrange("l t (f p) -> (l t f) p", p=P)).then_inc(rows_in, 16)
            sp.dma_start(rows[0:8, 2, :], c_ctx.rearrange("(k p) -> k p", p=P)).then_inc(rows_in, 16)
            sp.dma_start(rows[8:16, 2, :], c.rearrange("b (k p) -> (b k) p", p=P)).then_inc(rows_in, 16)
            sp.dma_start(const[:], tables).then_inc(consts_in, 16)

            def expert_slabs(i, l):
                for j in range(2):
                    e = l * EXPERTS + 2 * i + j
                    yield moe_w1.rearrange("l e (k p) n -> p (l e) k n", p=P)[:, bass.ds(e, 1)]
                    yield moe_w3.rearrange("l e (k p) n -> p (l e) k n", p=P)[:, bass.ds(e, 1)]
                    yield moe_w2.rearrange("l e (k p) n -> p (l e) k n", p=P)[:, bass.ds(e, 1)]

            def put(s, src, done):
                dst = slot(s).rearrange("p (o k n) -> p o k n", o=1, k=src.shape[2])
                sp.dma_start(dst, src).then_inc(done, 16)

            def slab_done(name):
                who, no = slab_job[name]
                sp.wait_ge({"dve": for_dve, "act": for_act, "ada": ada_full}[who], no)

            def moe_done(s, m, e):
                e = e + m // 3
                if m % 3 == 2:
                    sp.wait_ge(s["y_full"], e * 2 + 2)
                else:
                    sp.wait_ge(s["a_full"] if m % 3 == 0 else s["b_full"], e + 1)

            def store_y(s, e, rel, j, offset):
                sp.wait_ge(s["y"], e * 2 + 2)
                dst = expert_dram.rearrange("(e r) n -> r e n", r=CAP)[:, bass.ds(rel + offset * EXPERTS, 1)]
                sp.dma_start(dst, y_e[0:CAP, j, :].unsqueeze(1)).then_inc(s["y_stored"][j], 16)

            for l in range(DEPTH):
                for i, name in enumerate(PRE[l]):
                    s = pre_slot[name]
                    if i >= PRE_SLOTS:
                        slab_done(PRE[l][i - PRE_SLOTS])
                    elif l:
                        moe_done(es, MOE_SLOTS.index(s), l * EXPERTS - 2)
                    kind, layer, j = name
                    weights = {"ada": ada_w, "win": w_in, "wout": w_out}[kind]
                    src = weights[layer].rearrange("(k p) n -> p k n", p=P)[:, :, j * 512:(j + 1) * 512]
                    sp.dma_start(wide(s), src).then_inc(slab_in[s], 16)
                for m, src in enumerate(expert_slabs(0, l)):
                    s = MOE_SLOTS[m]
                    if s == 5:
                        sp.wait_ge(for_act, job["og", l, 2])
                    else:
                        slab_done([name for name in PRE[l] if pre_slot[name] == s][-1])
                    put(s, src, moe_in[m])
                with sp.Fori(1, EXPERTS // 2) as i:
                    for m, src in enumerate(expert_slabs(i, l)):
                        moe_done(es, m, i * 2 + (l * EXPERTS - 2))
                        put(MOE_SLOTS[m], src, moe_in[m])
                        if m % 3 == 2:
                            j = m // 3
                            store_y(es, i * 2 + (l * EXPERTS - 2 + j), i * 2 + (j - 2), j, 0)
                for j in range(2):
                    store_y(es, (l + 1) * EXPERTS - 2 + j, EXPERTS - 2 + j, j, 0)
                sp.wait_ge(counted, l + 1)
                top = sp.value_load(most[0:1, 0:1])
                with sp.If(top > CAP):
                    for again in range(OVER):
                        for m, src in enumerate(expert_slabs(0, l)):
                            if again:
                                moe_done(spare[l], m, again * EXPERTS - 2)
                            else:
                                moe_done(es, m, (l + 1) * EXPERTS - 2)
                            put(MOE_SLOTS[m], src, spare_in[l][m])
                        with sp.Fori(1, EXPERTS // 2) as i:
                            for m, src in enumerate(expert_slabs(i, l)):
                                moe_done(spare[l], m, i * 2 + (again * EXPERTS - 2))
                                put(MOE_SLOTS[m], src, spare_in[l][m])
                                if m % 3 == 2:
                                    j = m // 3
                                    store_y(spare[l], i * 2 + (again * EXPERTS - 2 + j), i * 2 + (j - 2), j,
                                            again + 1)
                        for j in range(2):
                            store_y(spare[l], (again + 1) * EXPERTS - 2 + j, EXPERTS - 2 + j, j, again + 1)
                    for m in range(6):
                        moe_done(spare[l], m, OVER * EXPERTS - 2)
            sp.wait_ge(x_ready, TILES * 2 * DEPTH)
            sp.dma_start(y_prompt[0], x[:, 0, :]).then_inc(out_stored, 16)
            sp.dma_start(y_sample.rearrange("b (t p) n -> p (b t) n", p=P), x[:, 1:3, :]).then_inc(out_stored, 16)
            sp.wait_ge(out_stored, 32 + 16 * len(debug or ()))
            sp.wait_ge(kv_stored, 32 * DEPTH)
            sp.wait_ge(state_out, 32 * DEPTH)
            for b in range(2):
                sp.wait_ge(es["y_stored"][b], 16 * DEPTH * EXPERTS // 2)

        @block.scalar
        def _(act):
            n = Counts()

            def filled(*name):
                act.wait_ge(for_act, job[name])
                return bank[4 + (job[name] - 1) % 3]

            def link(ins):
                ins.then_inc(act_step, 1)
                act.wait_ge(act_step, n(act_step))

            def f(out, in_, func=ACT.Copy, **kw):
                return nc.scalar.activation(out, in_, func, **kw)

            act.dma_start(x[:, 0, :], x_prompt[0]).then_inc(x_in, 16)
            act.dma_start(x[:, 1:3, :], x_sample.rearrange("b (t p) n -> p (b t) n", p=P)).then_inc(x_in, 16)
            for l in range(DEPTH):
                act.dma_start(w_ba[:, l], w_in[l].rearrange("(k p) n -> p k n", p=P)[:, :, N_IN - BA:N_IN]).then_inc(weights_in, 16)
                act.dma_start(w_rt[:, l, :, 0:4], moe_w_rg[l].rearrange("(k p) n -> p k n", p=P)).then_inc(weights_in, 16)
                act.dma_start(w_rt[:, l, :, 4:20], moe_w_re[l].rearrange("(k p) n -> p k n", p=P)).then_inc(weights_in, 16)
            for dst, src in (
                    (b_rt[:, :, 0:4], moe_b_rg), (b_rt[:, :, 4:20], moe_b_re),
                    (head_g[:, :, 0, :], na_qn_g), (head_g[:, :, 1, :], na_kn_g), (gdn_g[:], gdn_norm_g),
                    (gate_c[:, :, 0, :], gdn_a_log.rearrange("l d h -> l (d h)")),
                    (gate_c[:, :, 1, :], gdn_dt_bias.rearrange("l d h -> l (d h)"))):
                act.dma_start(dst, src.unsqueeze(0).broadcast_to([P] + list(src.shape))).then_inc(weights_in, 16)
            act.wait_ge(consts_in, 16)
            eps, one = tab("eps"), ones[:, 0:1]
            act.wait_ge(dve_emptied, job["cols",])
            f(silu_c[:], cols[:, 2, 0:16], ACT.Exp, scale=-1.0).then_inc(c_exp, 1)

            def inverse_root(dst, src, scale):
                act.wait_ge(ln_asked, n(ln_asked))
                link(f(dst, src, ACT.Ln, scale=scale, bias=eps))
                f(dst, dst, ACT.Exp, scale=-0.5).then_inc(rs_ready, 1)

            def norm(l, which):
                buf = (xn, xn2)[which - 1]
                for t in range(TILES):
                    if l == 0 and which == 1:
                        act.wait_ge(x_in, 32)
                    else:
                        act.wait_ge(x_ready, 6 * l + 3 * (which - 2) + t + 1)
                    if t == 2:
                        act.wait_ge(for_dve, job["norm", l, which, 0, 1])
                    link(f(buf[:, t % 2, :], x[:, t, :], ACT.Square, accum_out=ss[:, t:t + 1]))
                    link(f(rstd[:, t:t + 1], ss[:, t:t + 1], ACT.Ln, scale=1.0 / D, bias=eps))
                    link(f(rstd[:, t:t + 1], rstd[:, t:t + 1], ACT.Exp, scale=-0.5))
                    f(buf[:, t % 2, :], x[:, t, :], scale=rstd[:, t:t + 1]).then_inc(xn_ready, 1)

            for l in range(DEPTH):
                if l:
                    act.wait_ge(x_ready, 6 * l)
                norm(l, 1)

                def token_tile(which, t):
                    b = filled("win", l, which, t)
                    j = 3 * which + t
                    if which == 2:
                        f(v_sb[:, t, :], b[:]).then_inc(act_emptied, 1)
                        return
                    f((z, z_k)[which][:, t, :], b[:])
                    if j >= 2:
                        act.wait_ge(ln_asked, 12 * l + j - 1)
                    f(sq[:, j % 2, :], b[:], ACT.Square).then_inc(act_emptied, 1)

                def qk_cols(which, t):
                    b = filled("qkT", l, which, t)
                    dst = (qT, kT)[which]
                    f(dst[:, :, t * P:(t + 1) * P], b[:].rearrange("p (h n) -> p h n", h=4)).then_inc(act_emptied, 1)

                for which in range(3):
                    for t in range(TILES):
                        j = 3 * which + t
                        token_tile(which, t)
                        if 1 <= j <= 6:
                            inverse_root(hr[:, (j - 1) % 2, :], hss[:, (j - 1) % 2, :], 1.0 / HD)
                        if which:
                            qk_cols(which - 1, t)
                b = filled("past", l)
                f(kT[:, :, TOK:512], b[:].rearrange("p (h n) -> p h n", h=4)).then_inc(act_emptied, 1)

                act.wait_ge(pads_ready, l + 1)

                def conv_finish(c):
                    act.wait_ge(conv_ready, 12 * l + c + 1)
                    f(conv_acc[:, c % 2, :], conv_acc[:, c % 2, :], ACT.Silu).then_inc(silu_ready, 1)
                    b = filled("conv_back", l, c)
                    f(gq[:, :, c // 4, c % 4, :], b[:, 0:TOK].rearrange("p (t n) -> p t n", t=TILES)).then_inc(act_emptied, 1)

                for c in range(12):
                    b = filled("conv", l, c)
                    if c >= 2:
                        act.wait_ge(conv_ready, 12 * l + c - 1)
                    f(conv_in[:, c % 2, 2:2 + CTX], b[:, 0:CTX])
                    f(conv_in[:, c % 2, CTX + 6:CTX + 6 + LAT], b[:, CTX:TOK]).then_inc(act_emptied, 1)
                    if c:
                        conv_finish(c - 1)
                conv_finish(11)
                for t in range(TILES):
                    b = filled("win", l, 6, t)
                    f(zg[:, t, :], b[:], ACT.Silu).then_inc(act_emptied, 1)
                act.wait_ge(gates_x, l + 1)
                link(f(gabs, gabs, ACT.Exp, scale=-1.0))
                f(gabs, gabs, ACT.Ln, bias=one)
                f(beta, ba[:, :, 0:8], ACT.Exp, scale=-1.0)
                f(ea, gate_c[:, l, 0, :], ACT.Exp).then_inc(gates_e, 1)
                def probs(u):
                    t, h = divmod(u, HEADS)
                    keys = CTX if t == 0 else LAT + PAST
                    b = filled("score", l, u)
                    act.wait_ge(s_ready, 24 * l + u + 1)
                    f(p_sb[:, u % 2, 0:keys], b[:, 0:keys], ACT.Exp, bias=neg_max[:, t, h:h + 1],
                      accum_out=row_sum[:, t, h:h + 1]).then_inc(act_emptied, 1)

                def probs_T(u):
                    keys = CTX if u < HEADS else LAT + PAST
                    b = filled("probs", l, u)
                    if l or u >= 2:
                        act.wait_ge(pv_done, 24 * l + u - 1)
                    f(pT[:, u % 2, 0:keys], b[:, 0:keys]).then_inc(act_emptied, 1)

                def mixed_T(name, t, k0):
                    b = filled(name, l, t)
                    f(hT[:, k0:k0 + 4, t * P:(t + 1) * P], b[:].rearrange("p (k n) -> p k n", k=4)).then_inc(act_emptied, 1)

                probs(0)
                for u in range(TILES * HEADS):
                    if u + 1 < TILES * HEADS:
                        probs(u + 1)
                    probs_T(u)
                    if u in NORM_AT:
                        t = NORM_AT.index(u)
                        inverse_root(qr[:, t, :], qss[:, t, :], 1.0)
                    if u > 2 and u % 8 == 2:
                        mixed_T("o_na", u // 8 - 1, 0)
                mixed_T("o_na", 2, 0)

                for step in range(3):
                    for d in range(2):
                        b = filled("dt", l, step, d)
                        f(flat(gb[d][1]), b[:], ACT.Exp).then_inc(act_emptied, 1)
                        act.wait_ge(gsum_ready, n(gsum_ready))
                        f(gexp[d], gsum[d], ACT.Exp).then_inc(gexp_ready, 1)
                    for d in range(2):
                        for m, dst in enumerate((8, 10, 9, 5)):
                            b = filled("gT", l, step, d, m)
                            f(flat(gb[d][dst]), b[:]).then_inc(act_emptied, 1)
                    for level in range(1, LEVELS):
                        for d in range(2):
                            b = filled("at", l, step, level, d)
                            f(flat(gb[d][1]), b[:]).then_inc(act_emptied, 1)
                    for d in range(2):
                        b = filled("wT", l, step, d)
                        f(flat(gb[d][8]), b[:]).then_inc(act_emptied, 1)
                    for t in OUTS[step]:
                        inverse_root(orr, oss, 1.0 / GD)
                        mixed_T("og", t, 4)

                norm(l, 2)
                for t in range(TILES):
                    for half in range(2):
                        b = filled("tok", l, t, half)
                        f(tok_sb[:, t, half * 512:(half + 1) * 512], b[:]).then_inc(act_emptied, 1)
                act.wait_ge(router_x, l + 1)
                f(r_exp, r_exp, ACT.Exp).then_inc(router_e, 1)

                def run_experts(s, first):
                    def tokens_T(e, j, first_ever=False):
                        for half in range(2):
                            act.wait_ge(s["transposed"], e * 2 + half + 1)
                            if not first_ever:
                                act.wait_ge(s["b_full"], e - 1)
                            f(xT_e[:, j, 4 * half:4 * half + 4, :],
                              bank[half][:].rearrange("p (k n) -> p k n", k=4)).then_inc(s["xT"], 1)

                    def silu(e, j, first_ever=False):
                        act.wait_ge(s["a_full"], e + 1)
                        if not first_ever:
                            act.wait_ge(s["h"], e - 1)
                        f(silu_a[:, j, :], bank[2 + j][:], ACT.Silu).then_inc(s["silu"], 1)

                    def h_T(e, j):
                        act.wait_ge(s["hTp"], e + 1)
                        f(hT_e[:, j, :, :], bank[0][:].rearrange("p (k n) -> p k n", k=4)).then_inc(s["hT"], 1)

                    tokens_T(first, 0, first == 0)
                    silu(first, 0, first == 0)
                    tokens_T(first + 1, 1, first == 0)
                    silu(first + 1, 1, first == 0)
                    h_T(first, 0)
                    with act.Fori(1, EXPERTS // 2) as i:
                        e = i * 2 + first
                        tokens_T(e, 0)
                        silu(e, 0)
                        h_T(e - 1, 1)
                        tokens_T(e + 1, 1)
                        silu(e + 1, 1)
                        h_T(e, 0)
                    h_T(first + EXPERTS - 1, 1)

                run_experts(es, l * EXPERTS)
                act.wait_ge(counted, l + 1)
                top = act.value_load(most[0:1, 0:1])
                with act.If(top > CAP):
                    for again in range(OVER):
                        run_experts(spare[l], again * EXPERTS)

                for t in range(TILES):
                    act.wait_ge(y_in[t], 32 * (l + 1))
                    f(y_first[:, t, :], y_first[:, t, :], scale=w_tok[:, t, 0:1]).then_inc(combine_a, 1)

        @block.vector
        def _(dve):
            n = Counts()
            vec = nc.vector
            last_job = [0]

            def filled(*name):
                assert job[name] == last_job[0] + 1, name
                last_job[0] += 1
                dve.wait_ge(for_dve, job[name])
                return bank[(job[name] - 1) % 3]

            def link(ins):
                ins.then_inc(dve_step, 1)
                dve.wait_ge(dve_step, n(dve_step))

            def tt(out, a, b, op=ALU.mult):
                return vec.tensor_tensor(out, a, b, op)

            def ts(out, a, s1, s2=None, op0=ALU.mult, op1=None):
                if op1 is None:
                    return vec.tensor_scalar(out, a, s1, None, op0)
                return vec.tensor_scalar(out, a, s1, s2, op0, op1)

            def stt(out, a, s, b, op0, op1):
                return vec.scalar_tensor_tensor(out, a, s, b, op0, op1)

            b = filled("cols")
            vec.tensor_copy(cols[:, 0, :], b[:, 0:P])
            vec.tensor_copy(cols[:, 1, 0:120], b[:, P:P + 120])
            vec.tensor_copy(cols[:, 2, 0:16], b[:, 256:272]).then_inc(dve_emptied, 1)
            dve.wait_ge(consts_in, 16)
            vec.tensor_copy(tokid_b[:], tab("tokid"))
            dve.wait_ge(c_exp, 1)
            link(ts(silu_c[:], silu_c[:], 1.0, op0=ALU.add))
            link(vec.reciprocal(silu_c[:], silu_c[:]))
            tt(silu_c[:], silu_c[:], cols[:, 2, 0:16]).then_inc(silu_c_ready, 1)
            dve.wait_ge(weights_in, 16 * N_SMALL)

            def gate_rows(l, which, chunk):
                for s in range(2):
                    for half in range(2):
                        c0 = chunk * KC + 4 * half
                        if s:
                            dve.wait_ge(for_dve, job["gate", l, which, 0, half])
                        tt(silu_a[:, half, :].rearrange("p (q n) -> p q n", q=4), heads(ident, 4),
                           over(mods[:, l, c0:c0 + 4, s], P)).then_inc(diag_ready, 1)
                    for half in range(2):
                        b = filled("gate", l, which, s, half)
                        vec.tensor_copy(gate_b[:, s, half * 512:(half + 1) * 512], b[:]).then_inc(dve_emptied, 1)


            def ada_row(slab):
                no = slab_job[slab][1]
                dve.wait_ge(ada_full, no)
                vec.tensor_copy(mrow[:, (no - 1) % 2, :], bank[3][0:2, :]).then_inc(ada_taken, 1)

            def ada_col(slab):
                _, layer, i = slab
                b = filled("mod_col", *slab)
                tt(mods[:, layer, 4 * i:4 * i + 4, :], b[:, 0:8].rearrange("p (q s) -> p q s", s=2),
                   over(cols[:, 0, 48 * layer + 4 * i:48 * layer + 4 * i + 4], 2), ALU.add).then_inc(dve_emptied, 1)
                if i in (3, 9):
                    dve.wait_ge(dve_emptied, job[("mod_col", *slab)])
                    m, g0 = (1, 96) if i == 3 else (4, 112)
                    part = mods[:, layer, m * KC:(m + 1) * KC, :]
                    link(stt(part, part, 1.0, over(cols[:, 0, g0 + KC * layer:g0 + KC * layer + KC], 2),
                             ALU.add, ALU.mult))

            for i in range(EARLY):
                ada_row(("ada", 0, i))
                if i:
                    ada_col(("ada", 0, i - 1))
            ada_col(("ada", 0, EARLY - 1))
            for l in range(DEPTH):
                mod = mods[:, l]
                plan = mixing_plan([name for name in PRE[l][EARLY if l == 0 else 0:] if name[0] == "ada"])

                def point(p):
                    _, rows_, cols_ = plan[p]
                    for slab in cols_:
                        ada_col(slab)
                    for slab in rows_:
                        ada_row(slab)

                def modulated(which):
                    shift, scale = ((0, 1), (3, 4))[which - 1]
                    for t in range(TILES):
                        s = STREAM[t]
                        for half in range(2):
                            b = filled("norm", l, which, t, half)
                            for q in range(4):
                                k = 4 * half + q
                                last = ts(hT[:, k, t * P:(t + 1) * P], b[:, q * P:(q + 1) * P],
                                          mod[:, scale * KC + k, s:s + 1], mod[:, shift * KC + k, s:s + 1],
                                          ALU.mult, ALU.add)
                            last.then_inc(dve_emptied, 1)

                modulated(1)
                for j in range(6):
                    which, t = divmod(j, 3)
                    dst = (z, z_k)[which][:, t, :]
                    dst3 = dst.rearrange("p (h n) -> p h n", h=HEADS)
                    dve.wait_ge(act_emptied, job["win", l, which, t])
                    vec.reduce_sum(hss[:, j % 2, :], sq[:, j % 2, :].rearrange("p (h n) -> p h n", h=HEADS),
                                   AX).then_inc(ln_asked, 1)
                    dve.wait_ge(rs_ready, 12 * l + j + 1)
                    link(tt(dst3, dst3, over(hr[:, j % 2, :], HD)))
                    stt(dst3, dst3, (HD ** -0.5, 1.0)[which], heads(head_g[:, l, which, :], HEADS),
                        ALU.mult, ALU.mult).then_inc(zn_ready, 1)

                for c in range(12):
                    acc, src = conv_acc[:, c % 2, :], conv_in[:, c % 2, :]
                    dve.wait_ge(act_emptied, job["conv", l, c])
                    if c >= 2:
                        dve.wait_ge(for_act, job["conv_back", l, c - 2])
                    for tap in range(CONV):
                        w = cols[:, 1, 60 * l + 12 * tap + c:60 * l + 12 * tap + c + 1]
                        if tap == 0:
                            link(ts(acc, src[:, 0:CO], w))
                        elif tap < CONV - 1:
                            link(stt(acc, src[:, tap:tap + CO], w, acc, ALU.mult, ALU.add))
                        else:
                            stt(acc, src[:, tap:tap + CO], w, acc, ALU.mult, ALU.add).then_inc(conv_ready, 1)
                b = filled("ba", l)
                vec.tensor_copy(ba, b[:, 0:48].rearrange("p (t n) -> p t n", t=TILES)).then_inc(dve_emptied, 1)
                dve.wait_ge(dve_emptied, job["ba", l])
                link(tt(ga, ba[:, :, 8:16], heads(gate_c[:, l, 1, :], TILES), ALU.add))
                stt(gabs, ga, -1.0, ga, ALU.mult, ALU.max).then_inc(gates_x, 1)
                link(ts(ga, ga, 0.0, op0=ALU.max))
                dve.wait_ge(gates_e, l + 1)
                link(tt(ga, ga, gabs, ALU.add))
                link(stt(decay, ga, -1.0, heads(ea, TILES), ALU.mult, ALU.mult))
                link(ts(beta, beta, 1.0, op0=ALU.add))
                vec.reciprocal(beta, beta).then_inc(gates_ready, 1)
                def maxima(u):
                    t, h = divmod(u, HEADS)
                    keys = CTX if t == 0 else LAT + PAST
                    dve.wait_ge(for_act, job["score", l, u])
                    b = bank[4 + (job["score", l, u] - 1) % 3]
                    vec.tensor_reduce(neg_max[:, t, h:h + 1], b[:, 0:keys], AX, ALU.max, negate=True).then_inc(s_ready, 1)

                def outputs(t):
                    dve.wait_ge(pv_done, 24 * l + 8 * (t + 1))
                    if t:
                        dve.wait_ge(for_act, job["o_na", l, t - 1])
                    link(vec.reciprocal(row_sum[:, t, :], row_sum[:, t, :]))
                    tt(o_na.rearrange("p (h n) -> p h n", h=HEADS), bank[7][:].rearrange("p (h n) -> p h n", h=HEADS),
                       over(row_sum[:, t, :], HD)).then_inc(o_na_ready, 1)

                for u in range(TILES * HEADS):
                    maxima(u)
                    if u > 8 and u % 8 == 1:
                        outputs(u // 8 - 1)
                    if u in NORM_AT:
                        t = NORM_AT.index(u)
                        dve.wait_ge(sq_ready, 3 * l + t + 1)
                        vec.reduce_sum(qss[:, t, :], sq8, AX).then_inc(ln_asked, 1)
                    if u >= 2:
                        point(u - 2)
                point(22)
                point(23)
                outputs(2)

                incl = [tab("le"), tab("ge")]
                dve.wait_ge(for_act, job["o_na", l, 2])
                dve.wait_ge(gates_ready, l + 1)
                dve.wait_ge(gq_normed, 3 * l + 3)
                for step in range(3):
                    for d in range(2):
                        b = filled("gsum", l, step, d)
                        vec.tensor_copy(gsum[d][:, 0:8], b[:, 0:8]).then_inc(dve_emptied, 1)
                        dve.wait_ge(dve_emptied, job["gsum", l, step, d])
                        tt(gsum[d][:, 8:12], gsum[d][:, 4:8], gsum[d][:, 0:4], ALU.subtract).then_inc(gsum_ready, 1)
                    for d in range(2):
                        t = CHUNKS[step][d]
                        q_, k_ = gq[:, t, 0], gq[:, t, 1]
                        bt = over(beta[:, t, 4 * d:4 * d + 4], GD)
                        dve.wait_ge(gexp_ready, 6 * l + 2 * step + d + 1)
                        tt(gb[d][4], q_, over(gexp[d][:, 0:4], GD))
                        link(tt(gb[d][2], k_, bt))
                        stt(gb[d][3], gb[d][2], -1.0, over(gexp[d][:, 0:4], GD), ALU.mult, ALU.mult).then_inc(gdn_scaled, 1)
                        dve.wait_ge(act_emptied, job["dt", l, step, d])
                        link(tt(gb[d][1], gb[d][1], heads(incl[d], GH)))
                    for d in range(2):
                        for name, dst in (("qk", 9), ("kk", 10)):
                            b = filled(name, l, step, d)
                            tt(gb[d][dst], b[:].rearrange("p (h n) -> p h n", h=GH), gb[d][1]).then_inc(dve_emptied, 1)
                    for d in range(2):
                        dve.wait_ge(lvl_ready, 42 * l + 14 * step + d + 1)
                        tt(gb[d][4], heads(ident, GH), gb[d][0], ALU.subtract)
                        b = filled("t0", l, step, d)
                        tt(gb[d][2], heads(ident, GH), b[:].rearrange("p (h n) -> p h n", h=GH),
                           ALU.subtract).then_inc(dve_emptied, 1)
                    for level in range(1, LEVELS):
                        point(24 + 12 * step + 2 * (level - 1))
                        for d in range(2):
                            if level == 1:
                                dve.wait_ge(dve_emptied, job["t0", l, step, d])
                            else:
                                dve.wait_ge(dve_emptied, job["tu", l, step, level - 1, d])
                            for name, dst in ((("tat", 2),) if level < LEVELS - 1 else ()) + (("tu", 4),):
                                b = filled(name, l, step, level, d)
                                tt(gb[d][dst], gb[d][dst], b[:].rearrange("p (h n) -> p h n", h=GH),
                                   ALU.subtract).then_inc(dve_emptied, 1)
                        point(24 + 12 * step + 2 * (level - 1) + 1)
                    for d in range(2):
                        b = filled("vnew", l, step, d)
                        vec.tensor_copy(flat(gb[d][0]), b[:]).then_inc(dve_emptied, 1)
                    for d in range(2):
                        t = CHUNKS[step][d]
                        acc = o_acc[:, max(t - 1, 0), :]
                        b = filled("o", l, step, d)
                        if (step, d) in ((0, 0), (1, 0), (1, 1)):
                            vec.tensor_copy(acc, b[:]).then_inc(dve_emptied, 1)
                        else:
                            dve.wait_ge(dve_emptied, job["o", l, step, d] - 1)
                            tt(acc, acc, b[:], ALU.add).then_inc(dve_emptied, 1)
                        b = filled("kv", l, step, d)
                        for h in range(GH):
                            last = stt(state[d][:, h, :], state[d][:, h, :], gexp[d][:, 4 + h:5 + h],
                                       b[:, h * P:(h + 1) * P], ALU.mult, ALU.add)
                        last.then_inc(dve_emptied, 1)
                    dve.wait_ge(dve_emptied, job["kv", l, step, 1])
                    for t in OUTS[step]:
                        acc = o_acc[:, max(t - 1, 0), :]
                        acc3 = acc.rearrange("p (h n) -> p h n", h=GH)
                        tmp = gb[1][1]
                        if t == 2:
                            dve.wait_ge(for_act, job["og", l, 1])
                        link(tt(tmp, acc3, acc3))
                        vec.reduce_sum(oss, tmp, AX).then_inc(ln_asked, 1)
                        dve.wait_ge(rs_ready, 12 * l + 9 + t + 1)
                        link(tt(acc3, acc3, over(orr, GD)))
                        link(tt(acc3, acc3, heads(gdn_g[:, l, :], GH)))
                        tt(flat(tmp), acc, zg[:, t, :]).then_inc(og_ready, 1)

                dve.wait_ge(act_emptied, job["og", l, 2])
                gate_rows(l, 1, 2)
                dve.wait_ge(dve_emptied, job["gate", l, 1, 1, 1])
                for j in range(N_OUT):
                    for t in range(TILES):
                        b = filled("wout", l, j, t)
                        part = x[:, t, j * 512:(j + 1) * 512]
                        tt(silu_a[:, t % 2, :], b[:], gate_b[:, STREAM[t], j * 512:(j + 1) * 512]).then_inc(dve_emptied, 1)
                        dve.wait_ge(dve_emptied, job["wout", l, j, t])
                        ins = tt(part, part, silu_a[:, t % 2, :], ALU.add)
                        if j:
                            ins.then_inc(x_ready, 1)
                        else:
                            link(ins)
                modulated(2)

                b = filled("router", l)
                tt(lg, b[:, 0:60].rearrange("p (t n) -> p t n", t=TILES), heads(b_rt[:, l, :], TILES),
                   ALU.add).then_inc(dve_emptied, 1)
                dve.wait_ge(dve_emptied, job["router", l])

                def best(one_hot, top, values):
                    link(vec.reduce_max(top, values, AX))
                    link(tt(one_hot, values, over(top, 4), ALU.is_equal))
                    link(tt(one_hot, one_hot, heads(tab("first"), TILES)))
                    link(vec.reduce_max(t3, one_hot, AX))
                    link(tt(one_hot, one_hot, over(t3, 4), ALU.is_equal))

                best(oh_g, m_g, lg[:, :, 0:4])
                lg16 = lg[:, :, 4:20].rearrange("p t (g j) -> p t g j", g=4)
                t16v = t16.rearrange("p t (g j) -> p t g j", g=4)
                link(tt(t16v, lg16, oh_g.unsqueeze(3).broadcast_to([P, TILES, 4, 4])))
                link(vec.reduce_sum(el, t16.rearrange("p t (g j) -> p t j g", g=4), AX))
                best(oh1, m_1, el)
                link(stt(el, oh1, -BIG, el, ALU.mult, ALU.add))
                best(oh2, m_2, el)
                tt(r_exp[:, :, 0:4], lg[:, :, 0:4], over(m_g, 4), ALU.subtract)
                tt(r_exp[:, :, 4], m_2, m_1, ALU.subtract).then_inc(router_x, 1)
                for c_, oh in enumerate((oh1, oh2)):
                    for t in range(TILES):
                        ins = tt(choice[:, t, c_, :].rearrange("p (g j) -> p g j", g=4), over(oh_g[:, t, :], 4),
                                 heads(oh[:, t, :], 4))
                link(ins)
                tt(chosen, choice[:, :, 0, :], choice[:, :, 1, :], ALU.add).then_inc(routed, 1)
                dve.wait_ge(router_e, l + 1)
                link(vec.reduce_sum(t3, r_exp[:, :, 0:4], AX))
                link(vec.reciprocal(t3, t3))
                link(ts(m_1, r_exp[:, :, 4], 1.0, op0=ALU.add))
                link(vec.reciprocal(m_1, m_1))
                link(tt(w_tok[:, :, 0], t3, m_1))
                link(tt(w_tok[:, :, 1], w_tok[:, :, 0], r_exp[:, :, 4]))
                gate_rows(l, 2, 5)
                b = filled("place", l)
                vec.reduce_max(t1, b[:, 48:64], AX)
                vec.tensor_copy(place, b[:, 0:48].rearrange("p (t n) -> p t n", t=TILES)).then_inc(dve_emptied, 1)
                dve.wait_ge(dve_emptied, job["place", l])
                vec.tensor_copy(most[:], t1[0:1, :]).then_inc(counted, 1)
                link(stt(t16, heads(tab("row0"), TILES), float(CAP), place, ALU.mult, ALU.add))
                for again in range(1, OVER + 1):
                    link(ts(shifted, place, float(again * CAP), float((EXPERTS - 1) * CAP), ALU.is_ge, ALU.mult))
                    link(tt(t16, t16, shifted, ALU.add))
                for c_ in range(2):
                    link(tt(choice[:, :, c_, :], choice[:, :, c_, :], t16))
                    link(vec.reduce_sum(rowf[:, :, c_], choice[:, :, c_, :], AX))
                link(vec.tensor_copy(idx_row[:], rowf))
                link(ts(place, place, 1.0, op0=ALU.add))
                link(tt(place, place, chosen))
                link(ts(place, place, -1.0, op0=ALU.add))

                def run_experts(s, first, offset):
                    def link(ins):
                        ins.then_inc(s["step"], 1)
                        dve.wait_ge(s["step"], n(s["step"]))

                    link(ts(shifted, place, -float(offset), op0=ALU.add))
                    for group in range(4):
                        g = first // 4 + group
                        if g:
                            dve.wait_ge(s["list_full"], g)
                        for t in range(TILES):
                            ins = tt(sel[:, t, :, :], heads(tab("slot"), 4),
                                     over(shifted[:, t, 4 * group:4 * group + 4], P), ALU.is_equal)
                        ins.then_inc(s["sel"], 1)
                        dve.wait_ge(s["list_full"], g + 1)
                        link(vec.tensor_copy(pair_f, bank[6 + group % 2][:, 0:8]))
                        pf = pair_f.rearrange("p (e c) -> p e c", c=2)
                        stt(idx[:, 4 * group:4 * group + 4], pf[:, :, 1], float(P), pf[:, :, 0],
                            ALU.mult, ALU.add).then_inc(s["list_taken"], 1)
                        dve.wait_ge(s["list_taken"], g + 1)

                    def product(e, j, first_ever=False):
                        dve.wait_ge(s["silu"], e + 1)
                        dve.wait_ge(s["b_full"], e + 1)
                        if not first_ever:
                            dve.wait_ge(s["hTp"], e - 1)
                        tt(h_e[:, j, :], silu_a[:, j, :], bank[4 + j][:]).then_inc(s["h"], 1)

                    def result(e, j, pair, first_ever=False):
                        for half in range(2):
                            dve.wait_ge(s["y_full"], e * 2 + half + 1)
                            if not first_ever:
                                dve.wait_ge(s["y_stored"][j], 16 * pair)
                            vec.tensor_copy(y_e[:, j, half * 512:(half + 1) * 512], bank[6 + half][:]).then_inc(s["y"], 1)

                    pair = first // 2
                    product(first, 0, first == 0)
                    product(first + 1, 1, first == 0)
                    result(first, 0, pair, first == 0)

                    def two_experts(i, first_ever=False):
                        e = i * 2 + first
                        product(e, 0)
                        result(e - 1, 1, i + (pair - 1), first_ever)
                        product(e + 1, 1)
                        result(e, 0, i + pair)

                    two_experts(1, first == 0)
                    with dve.Fori(2, EXPERTS // 2) as i:
                        two_experts(i)
                    result(first + EXPERTS - 1, 1, pair + EXPERTS // 2 - 1)

                run_experts(es, l * EXPERTS, 0)
                top = dve.value_load(most[0:1, 0:1])
                with dve.If(top > CAP):
                    for again in range(OVER):
                        run_experts(spare[l], again * EXPERTS, (again + 1) * CAP)

                for t in range(TILES + 1):
                    if t < TILES:
                        dve.wait_ge(combine_a, 3 * l + t + 1)
                        a = y_first[:, t, :]
                        stt(a, y_second[:, t, :], w_tok[:, t, 1:2], a, ALU.mult, ALU.add).then_inc(combine_b, 1)
                    if t:
                        dve.wait_ge(combine_c, 3 * l + t)
                        tt(x[:, t - 1, :], x[:, t - 1, :], y_first[:, t - 1, :], ALU.add).then_inc(x_ready, 1)

        @block.gpsimd
        def _(pool):
            n = Counts()
            gp = nc.gpsimd

            def link(ins):
                ins.then_inc(pool_step, 1)
                pool.wait_ge(pool_step, n(pool_step))

            def tt(out, a, b, op=ALU.mult):
                return gp.tensor_tensor(out, a, b, op)

            pool.wait_ge(consts_in, 16)
            for l in range(DEPTH):
                if l:
                    pool.wait_ge(x_ready, 6 * l)
                pool.dma_start(k_past, cache_k[0, l].rearrange("s h d -> s (h d)")).then_inc(past_in, 16)
                pool.dma_start(v_past, cache_v[0, l].rearrange("s h d -> s (h d)")).then_inc(past_in, 16)
                pool.wait_ge(dve_emptied, job["norm", l, 1, 2, 1])
                gp.memset(conv_in, 0.0).then_inc(pads_ready, 1)
                pool.wait_ge(zn_ready, 6 * l + 4)
                pool.dma_start(new_k[0, l].rearrange("s h d -> s (h d)"), z_k[:, 0, :]).then_inc(kv_stored, 16)
                pool.wait_ge(act_emptied, job["win", l, 2, 0])
                pool.dma_start(new_v[0, l].rearrange("s h d -> s (h d)"), v_sb[:, 0, :]).then_inc(kv_stored, 16)
                pool.wait_ge(kv_stored, 32 * (l + 1))
                pool.wait_ge(for_act, job["qkT", l, 1, 2])
                def bias_lot(lot):
                    t, h4 = 1 + lot // 2, lot % 2
                    if lot >= 2:
                        pool.wait_ge(for_act, job["score", l, 8 * (t - 1) + 4 * h4 + 3])
                    for row in range(2):
                        q_row = 2 * (t - 1) + row
                        for h in range(4):
                            at = ((l * HEADS + 4 * h4 + h) * RPB_H + 7 - q_row) * RPB_W + NA_KW - GRID_W
                            src = bass.AP(na_rpb.tensor, at, [[1, GRID_W], [RPB_W, ROWS], [1, GRID_W]])
                            dst = bias[row * GRID_W:(row + 1) * GRID_W, h4, h, :].rearrange("p (r n) -> p r n", r=ROWS)
                            pool.dma_start(dst, src).then_inc(bias_in, 16)
                    pool.wait_ge(bias_in, 128 * (4 * l + lot + 1))
                    tt(bias[:, h4], bias[:, h4], heads(tab("window").rearrange("p r n -> p (r n)"), 4),
                       ALU.add).then_inc(bias_ready, 1)

                def lengths_and_turn(t):
                    qk = gq[:, t, 0:2].rearrange("p s h d -> p (s h) d")
                    tt(sq8, qk, qk).then_inc(sq_ready, 1)
                    pool.wait_ge(rs_ready, 12 * l + 6 + t + 1)
                    link(gp.tensor_scalar(qr[:, t, 0:4], qr[:, t, 0:4], GD ** -0.5, None, ALU.mult))
                    ins = tt(qk, qk, over(qr[:, t, :], GD))
                    if t:
                        link(ins)
                        v = qk.rearrange("p h (a b n) -> p h a b n", a=2, b=2)
                        x1, x2 = v[:, :, :, 0, :], v[:, :, :, 1, :]
                        cos_, sin_ = (tab(k)[:, t - 1].unsqueeze(1).broadcast_to([P, 8, 2, 32]) for k in ("cos", "sin"))
                        tt(turn[:, 0], x1, cos_)
                        tt(turn[:, 1], x2, sin_)
                        link(tt(turn[:, 2], x1, sin_))
                        link(tt(x1, turn[:, 0], turn[:, 1], ALU.subtract))
                        link(tt(turn[:, 0], x2, cos_))
                        ins = tt(x2, turn[:, 2], turn[:, 0], ALU.add)
                    ins.then_inc(gq_normed, 1)
                    pool.wait_ge(gq_normed, 3 * l + t + 1)

                bias_lot(0)
                bias_lot(1)
                pool.wait_ge(act_emptied, job["conv_back", l, 11])
                lengths_and_turn(0)
                lengths_and_turn(1)
                bias_lot(2)
                lengths_and_turn(2)
                bias_lot(3)

                pool.wait_ge(for_act, job["o_na", l, 2])
                for d in range(2):
                    gp.memset(state[d], 0.0).then_inc(state_zero, 1)
                pool.wait_ge(gates_ready, l + 1)
                incl = [tab("le"), tab("ge")]
                for step in range(3):
                    for d in range(2):
                        t = CHUNKS[step][d]
                        if step:
                            pool.wait_ge(for_dve, job["kv", l, step - 1, d])
                        tt(gb[d][0], heads(incl[d], GH), over(decay[:, t, 4 * d:4 * d + 4], P)).then_inc(decay_rhs, 1)
                    for d in range(2):
                        t = CHUNKS[step][d]
                        tt(gb[d][7], gq[:, t, 2], over(beta[:, t, 4 * d:4 * d + 4], GD))
                        pool.wait_ge(gexp_ready, 6 * l + 2 * step + d + 1)
                        tt(gb[d][6], gq[:, t, 1], over(gexp[d][:, 8:12], GD)).then_inc(pool_scaled, 1)
                    for level in range(LEVELS):
                        for d in range(2):
                            if level == 0:
                                pool.wait_ge(dve_emptied, job["kk", l, step, d])
                            elif level == 1:
                                pool.wait_ge(dve_emptied, job["t0", l, step, d])
                            else:
                                pool.wait_ge(for_act, job["at", l, step, level - 1, d])
                            tt(gb[d][0], gb[d][10], heads(tab("levels")[:, d, level, :], GH)).then_inc(lvl_ready, 1)
                    if step == 0:
                        for d in range(2):
                            pool.wait_ge(dve_emptied, job["kv", l, 0, d])
                            pool.dma_start(new_state[0, l, d].rearrange("h k v -> k h v"), state[d]).then_inc(state_out, 16)
                        pool.wait_ge(state_out, 32 * (l + 1))
                        for d in range(2):
                            pool.dma_start(state[d], state_ssm[0, l, d].rearrange("h k v -> k h v")).then_inc(state_in, 16)

                for t in range(TILES):
                    pool.wait_ge(act_emptied, job["tok", l, t, 1])
                    pool.dma_start(tok_dram[t * P:(t + 1) * P, :], tok_sb[:, t, :]).then_inc(tok_stored, 16)
                pool.wait_ge(tok_stored, 48 * (l + 1))

                def run_experts(s, first):
                    pool.wait_ge(s["list_taken"], first // 4 + 4)

                    def gather(e, rel, j, first_ever=False):
                        if not first_ever:
                            pool.wait_ge(s["transposed"], e * 2 - 2)
                        gp.tensor_copy(idx_now[:, j:j + 1], idx[:, bass.ds(rel, 1)]).then_inc(s["idx_copied"], 1)
                        pool.wait_ge(s["idx_copied"], e + 1)
                        pool.sem_inc(s["gathering"])
                        pool.indirect_dma_start(
                            out=x_e[:, j, :], out_offset=None, in_=tok_dram,
                            in_offset=bass.IndirectOffsetOnAxis(ap=idx_now[:, j:j + 1], axis=0)).then_inc(s["gathered"][j], 16)

                    gather(first, 0, 0, first == 0)
                    gather(first + 1, 1, 1, first == 0)
                    with pool.Fori(1, EXPERTS // 2) as i:
                        gather(i * 2 + first, i * 2, 0)
                        gather(i * 2 + (first + 1), i * 2 + 1, 1)

                run_experts(es, l * EXPERTS)
                for b in range(2):
                    pool.wait_ge(es["y_stored"][b], 16 * (l + 1) * EXPERTS // 2)

                def gather_rows(rows_):
                    for t in range(TILES):
                        for c_, dst in enumerate((y_first, y_second)):
                            pool.indirect_dma_start(
                                out=dst[:, t, :], out_offset=None, in_=expert_dram[0:rows_, :],
                                in_offset=bass.IndirectOffsetOnAxis(ap=idx_row[:, t, c_:c_ + 1], axis=0)
                            ).then_inc(y_in[t], 16)

                pool.wait_ge(counted, l + 1)
                top = pool.value_load(most[0:1, 0:1])
                with pool.If(top > CAP):
                    for again in range(OVER):
                        run_experts(spare[l], again * EXPERTS)
                    for b in range(2):
                        pool.wait_ge(spare[l]["y_stored"][b], 16 * OVER * EXPERTS // 2)
                    gather_rows((1 + OVER) * EXPERTS * CAP)
                with pool.If(top < CAP + 1):
                    gather_rows(EXPERTS * CAP)
                for t in range(TILES):
                    pool.wait_ge(combine_b, 3 * l + t + 1)
                    tt(y_first[:, t, :], y_first[:, t, :], gate_b[:, STREAM[t], :]).then_inc(combine_c, 1)


_INS = ["x_prompt", "x_sample", "c", "cache_k", "cache_v", "state_ssm", "c_ctx", "ada_w", "ada_b", "norm1_g",
        "norm2_g", "w_in", "w_out", "na_qn_g", "na_kn_g", "na_rpb", "gdn_conv_w", "gdn_a_log", "gdn_dt_bias",
        "gdn_norm_g", "moe_w_rg", "moe_b_rg", "moe_w_re", "moe_b_re", "moe_w1", "moe_w3", "moe_w2"]
_OUTS = [(1, CTX, D), (1, LAT, D), (1, DEPTH, CTX, HEADS, HD), (1, DEPTH, CTX, HEADS, HD),
         (1, DEPTH, 2, GH, GD, GD)]


def kernel(**inputs):
    import concourse.bacc as _bacc
    from concourse.bass_utils import run_bass_kernel_spmd as _run

    nc = _bacc.Bacc("TRN2", target_bir_lowering=False, num_devices=1)
    where, tables = constants()
    arrays, args = {}, []
    for name in _INS:
        a = np.ascontiguousarray(inputs[name])
        arrays[f"in_{name}_dram"] = a
        args.append(nc.dram_tensor(f"in_{name}_dram", a.shape, mybir.dt.from_np(a.dtype), kind="ExternalInput").ap())
    arrays["in_tables_dram"] = tables
    args.append(nc.dram_tensor("in_tables_dram", tables.shape, F32, kind="ExternalInput").ap())
    for i, shape in enumerate(_OUTS):
        args.append(nc.dram_tensor(f"out_{i}_dram", shape, F32, kind="ExternalOutput").ap())
    program(nc, *args, where)
    r = _run(nc, [arrays], core_ids=[0])
    return tuple(r.results[0][f"out_{i}_dram"] for i in range(len(_OUTS)))
```

```python
from contextlib import ExitStack

import concourse.bass as bass
import numpy as np
from concourse import mybir

ALU = mybir.AluOpType
ACT = mybir.ActivationFunctionType
F32 = mybir.dt.float32
BF16 = mybir.dt.bfloat16
I32 = mybir.dt.int32
U32 = mybir.dt.uint32
AX = mybir.AxisListType.X

P = 128
D = 1024
KC = D // P
CTX, LAT, PAST = 128, 256, 128
TOK = CTX + LAT
TILES = TOK // P
STREAM = [0, 1, 1]
DEPTH = 2
HEADS, HD = 8, 64
GRID_W, ROWS, NA_KW = 64, LAT // 64, 16
RPB_H, RPB_W = 15, 31
GH, GD = 4, 128
CONV = 5
N_IN = 3600
BA = 4 * GH
EXPERTS, GROUPS, PER = 16, 4, 4
EPS = 1e-6
BIG = 1.0e30
SLAB = 4096
N_ADA, N_WIN, N_OUT = 12, 7, 2
EARLY = 4
PRE_SLOTS = 5
MOE_SLOTS = [1, 2, 3, 5, 4, 0]
STEP_WEIGHTS = [3.0, 2.0, 1.0] + 12 * [0.7] + [1.0, 1.0]
WEIGHTS = 24 * [0.8] + 3 * STEP_WEIGHTS
POINTS = len(WEIGHTS)
NORM_AT = [2, 9, 16]
CHUNKS = [(0, 0), (1, 2), (2, 1)]
OUTS = [[0], [], [2, 1]]
N_SMALL = 3 * DEPTH + 7
N_SCRAP = 920
LEVELS = 7


def constants():
    t = np.arange(P)
    parts = {
        "ident": np.eye(P),
        "ones": np.ones((P, P)),
        "le": t[:, None] <= t[None, :],
        "ge": t[:, None] >= t[None, :],
        "gt": t[:, None] > t[None, :],
        "lt": t[:, None] < t[None, :],
    }
    levels = np.zeros((P, 2, LEVELS, P))
    for level in range(LEVELS):
        half = 1 << level
        block, upper = t // (2 * half), (t // half) % 2
        same = block[:, None] == block[None, :]
        levels[:, 0, level] = same & (upper[:, None] == 0) & (upper[None, :] == 1)
        levels[:, 1, level] = same & (upper[:, None] == 1) & (upper[None, :] == 0)
    parts["levels"] = levels
    half = GD // 2
    freq = (10000.0 ** (-np.arange(0, half, 2, dtype=np.float32) / np.float32(half))).astype(np.float32)
    tok = np.arange(LAT)
    cos, sin = np.zeros((P, 2, 2, 32), np.float32), np.zeros((P, 2, 2, 32), np.float32)
    for tile in range(2):
        for axis, pos in enumerate((tok // GRID_W, tok % GRID_W)):
            ang = pos[tile * P:(tile + 1) * P].astype(np.float32)[:, None] * freq
            cos[:, tile, axis], sin[:, tile, axis] = np.cos(ang), np.sin(ang)
    parts["cos"], parts["sin"] = cos, sin
    col = GRID_W - 1 - t % GRID_W
    parts["flip"] = (t[:, None] // GRID_W == t[None] // GRID_W) & (col[:, None] == t[None] % GRID_W)
    start = np.clip(col - NA_KW // 2, 0, GRID_W - NA_KW)
    kcol = np.arange(GRID_W)
    inside = (kcol[None] >= start[:, None]) & (kcol[None] < start[:, None] + NA_KW)
    parts["window"] = np.broadcast_to(np.where(inside, 0.0, -BIG)[:, None], (P, ROWS, GRID_W))
    parts["first"] = np.broadcast_to(4.0 - np.arange(4), (P, 4))
    parts["row0"] = np.broadcast_to(np.arange(EXPERTS) * 1.0, (P, EXPERTS))
    parts["slot"] = np.broadcast_to(t.astype(np.float64), (P, P))
    parts["tokid"] = np.stack([np.stack([t, np.full(P, tile)], 1) for tile in range(TILES)], 1)
    at, where, cols = 0, {}, []
    for name, a in parts.items():
        a = np.asarray(a, np.float32)
        where[name] = (at, a.shape[1:])
        cols.append(a.reshape(P, -1))
        at += cols[-1].shape[1]
    return where, np.ascontiguousarray(np.concatenate(cols, 1))


def pre_slabs():
    out = []
    for l in range(DEPTH):
        ada = [("ada", l, i) for i in range(EARLY, N_ADA)]
        if l + 1 < DEPTH:
            ada += [("ada", l + 1, i) for i in range(EARLY)]
        first = [("ada", 0, i) for i in range(EARLY)] if l == 0 else []
        out.append(first + [("win", l, j) for j in range(N_WIN)] + ada + [("wout", l, j) for j in range(N_OUT)])
    return out


def mixing_plan(slabs):
    products, rows_at, cols_at = [], [[] for _ in range(POINTS)], [[] for _ in range(POINTS)]
    todo = [(s, k) for s in slabs for k in range(KC)]
    share = len(todo) / sum(WEIGHTS[:-4])
    due, made = 0.0, 0
    for point in range(POINTS):
        due += share * WEIGHTS[point]
        now = []
        while todo and made < due - 1e-6:
            now.append(todo.pop(0))
            made += 1
            if now[-1][1] == KC - 1:
                break
        products.append(now)
        for s, k in now:
            if k == KC - 1:
                rows_at[point + 1].append(s)
                cols_at[point + 2].append(s)
    assert not todo
    return list(zip(products, rows_at, cols_at))


class Counts:

    def __init__(self):
        self.seen = {}

    def __call__(self, sem, more=1):
        self.seen[sem.name] = self.seen.get(sem.name, 0) + more
        return self.seen[sem.name]


def over(ap, n):
    return ap.unsqueeze(2).broadcast_to([ap.shape[0], ap.shape[1], n])


def heads(ap, n):
    return ap.unsqueeze(1).broadcast_to([ap.shape[0], n, ap.shape[1]])


def flat(a):
    return a.rearrange("p h n -> p (h n)")


def program(nc, x_prompt, x_sample, c, cache_k, cache_v, state_ssm, c_ctx, ada_w, ada_b, norm1_g,
            norm2_g, w_in, w_out, na_qn_g, na_kn_g, na_rpb, gdn_conv_w, gdn_a_log, gdn_dt_bias,
            gdn_norm_g, moe_w_rg, moe_b_rg, moe_w_re, moe_b_re, moe_w1, moe_w3, moe_w2, tables,
            y_prompt, y_sample, new_k, new_v, new_state, where, CAP=P):
    OVER = (TOK + CAP - 1) // CAP - 1
    ctx = ExitStack()
    with ctx:
        def sb(name, shape, dt=F32):
            return ctx.enter_context(nc.sbuf_tensor(name, shape, dt))

        def sem(name):
            return ctx.enter_context(nc.semaphore(name))

        bank = [ctx.enter_context(nc.psum_tensor(f"bank{i}", [P, 512], F32)) for i in range(8)]
        tok_dram = nc.dram_tensor("tok_dram", [TOK, D], F32, kind="Internal").ap()
        expert_dram = nc.dram_tensor("expert_dram", [(1 + OVER) * EXPERTS * CAP, D], F32, kind="Internal").ap()

        const = sb("const", list(tables.shape))
        ring = sb("ring", [P, PRE_SLOTS, SLAB])
        x = sb("x", [P, TILES, D])
        hT = sb("hT", [P, KC, TOK])
        cols = sb("cols", [P, 3, P])
        silu_c = sb("silu_c", [P, 16])
        mods = sb("mod", [P, DEPTH, 48, 2])
        mrow = sb("mrow", [2, 2, 512])
        w_ba = sb("w_ba", [P, DEPTH, KC, BA])
        w_rt = sb("w_rt", [P, DEPTH, KC, GROUPS + EXPERTS])
        b_rt = sb("b_rt", [P, DEPTH, GROUPS + EXPERTS])
        head_g = sb("head_g", [P, DEPTH, 2, HD])
        gdn_g = sb("gdn_g", [P, DEPTH, GD])
        gate_c = sb("gate_c", [P, DEPTH, 2, 8])
        small = sb("small", [P, N_SCRAP])
        idx = sb("idx", [P, EXPERTS], U32)
        idx_now = sb("idx_now", [P, 2], U32)
        idx_row = sb("idx_row", [P, TILES, 2], U32)
        most = sb("most", [1, 1], I32)
        tokid_b = sb("tokid_b", [P, TILES, 2], BF16)
        arena = sb("arena", [P, 19456])

        def tab(name):
            at, shape = where[name]
            size = int(np.prod(shape))
            flat = const[:, at:at + size]
            if len(shape) == 1:
                return flat
            names = "abcd"[:len(shape)]
            return flat.rearrange(f"p ({' '.join(names)}) -> p {' '.join(names)}",
                                  **{k: int(v) for k, v in zip(names, shape)})

        at_now = [0]

        def take(n, reset=None):
            if reset is not None:
                at_now[0] = reset
            at_now[0] += n
            assert at_now[0] <= 19456, at_now[0]
            return arena[:, at_now[0] - n:at_now[0]]

        ident, ones = tab("ident"), tab("ones")
        rows = take(3 * P, 0).rearrange("p (r n) -> p r n", r=3)
        gq = take(3 * 1536, 0).rearrange("p (t s h d) -> p t s h d", t=TILES, s=3, h=GH)
        zg = take(3 * 512).rearrange("p (t n) -> p t n", t=TILES)
        z = take(3 * 512, 6144).rearrange("p (t n) -> p t n", t=TILES)
        v_sb = take(3 * 512).rearrange("p (t n) -> p t n", t=TILES)
        v_past = take(512)
        k_past = take(512)
        qT = take(4 * TOK).rearrange("p (h n) -> p h n", h=4)
        kT = take(4 * 512).rearrange("p (h n) -> p h n", h=4)
        bias = take(2 * 1024).rearrange("p (b h n) -> p b h n", b=2, h=4)
        z_k = take(3 * 512, at_now[0] - 2048).rearrange("p (t n) -> p t n", t=TILES)
        at_now[0] += 512
        scratch = at_now[0]
        sq = take(1024).rearrange("p (b n) -> p b n", b=2)
        take(768)
        p_sb = take(768).rearrange("p (b n) -> p b n", b=2)
        pT = take(768).rearrange("p (b n) -> p b n", b=2)
        o_na = z[:, 0, :]
        sq8 = take(1024, scratch).rearrange("p (h n) -> p h n", h=8)
        turn = take(1536, scratch).rearrange("p (b h a n) -> p b h a n", b=3, h=8, a=2)
        diag1 = take(TILES * P, scratch).rearrange("p (t n) -> p t n", t=TILES)
        junk1 = take(512)
        CW = 2 + CTX + 2 + 2 + LAT + 2
        CO = CW - 4
        conv_in = take(2 * CW, scratch + 1024).rearrange("p (b n) -> p b n", b=2)
        conv_acc = take(2 * CO).rearrange("p (b n) -> p b n", b=2)
        take(0, 6144)
        gb = [[take(512).rearrange("p (h n) -> p h n", h=GH) for _ in range(11)] for _ in range(2)]
        state = [take(512).rearrange("p (h n) -> p h n", h=GH) for _ in range(2)]
        o_acc = take(1024).rearrange("p (t n) -> p t n", t=2)
        gate1 = [arena[:, 6144 + 11 * 512 * d + 512:6144 + 11 * 512 * d + 3 * 512] for d in range(2)]
        slot5 = take(SLAB, 0)
        x_e = take(2048).rearrange("p (b n) -> p b n", b=2)
        xT_e = take(2048).rearrange("p (b k n) -> p b k n", b=2, k=KC)
        silu_a = take(1024).rearrange("p (b n) -> p b n", b=2)
        h_e = take(1024).rearrange("p (b n) -> p b n", b=2)
        hT_e = take(1024).rearrange("p (b k n) -> p b k n", b=2, k=4)
        y_e = take(2048).rearrange("p (b n) -> p b n", b=2)
        diag2 = take(TILES * P, at_now[0] - 2048).rearrange("p (t n) -> p t n", t=TILES)
        junk2 = take(512)
        take(2048 - TILES * P - 512)
        sel = take(768).bitcast(BF16).rearrange("p (t e n) -> p t e n", t=TILES, e=4)
        sel = [sel, y_e[:, 1, 0:768].bitcast(BF16).rearrange("p (t e n) -> p t e n", t=TILES, e=4)]
        gate2 = take(2048).rearrange("p (s n) -> p s n", s=2)
        tok_sb = take(3072).rearrange("p (t n) -> p t n", t=TILES)
        y_first = hT[:].rearrange("p k n -> p (k n)").rearrange("p (t n) -> p t n", t=TILES)
        y_second = take(3072, SLAB).rearrange("p (t n) -> p t n", t=TILES)

        at_small = [0]

        def sm(n):
            at_small[0] += n
            assert at_small[0] <= N_SCRAP
            return small[:, at_small[0] - n:at_small[0]]

        def smt(n):
            return sm(TILES * n).rearrange("p (t n) -> p t n", t=TILES)

        ss = sm(2 * TILES).rearrange("p (t n) -> p t n", t=TILES)
        ssum, rstd = sm(TILES), sm(TILES)
        nv, ny, nt = sm(24), sm(24), sm(24)
        hss = sm(16).rearrange("p (b n) -> p b n", b=2)
        hr = sm(16).rearrange("p (b n) -> p b n", b=2)
        ba, beta, decay, ga, gabs, ea = smt(16), smt(8), smt(8), smt(8), smt(8), sm(8)
        qss, qr = smt(8), smt(8)
        neg_max, row_sum = smt(8), smt(8)
        gsum, gexp = [sm(12) for _ in range(2)], [sm(12) for _ in range(2)]
        oss, orr = sm(12).rearrange("p (t n) -> p t n", t=TILES), sm(12).rearrange("p (t n) -> p t n", t=TILES)
        lg, r_exp = smt(20), smt(5)
        m_g, m_1, m_2, t3 = (sm(TILES) for _ in range(4))
        oh_g, oh1, oh2, el = (smt(4) for _ in range(4))
        t16 = smt(16)
        w_tok, rowf = smt(2), smt(2)
        choice = sm(96).rearrange("p (t c n) -> p t c n", t=TILES, c=2)
        chosen, place, shifted = smt(16), smt(16), smt(16)
        pair_f, t1 = sm(8), sm(1)

        consts_in, rows_in, weights_in, x_in = map(sem, ("consts_in", "rows_in", "weights_in", "x_in"))
        dve_step, act_step, pool_step = map(sem, ("dve_step", "act_step", "pool_step"))
        for_dve, dve_emptied = sem("for_dve"), sem("dve_emptied")
        for_act, act_emptied = sem("for_act"), sem("act_emptied")
        ada_full, ada_taken = sem("ada_full"), sem("ada_taken")
        slab_in = [sem(f"slab_in{i}") for i in range(PRE_SLOTS)]
        moe_in = [sem(f"moe_in{i}") for i in range(6)]
        c_exp, silu_c_ready = sem("c_exp"), sem("silu_c_ready")
        ss_ready, scale_ready = sem("ss_ready"), sem("scale_ready")
        x_half, x_ready = sem("x_half"), sem("x_ready")
        zn_ready = sem("zn_ready")
        past_in, kv_stored = sem("past_in"), sem("kv_stored")
        bias_in, bias_ready = [sem(f"bias_in{i}") for i in range(2)], sem("bias_ready")
        s_ready = sem("s_ready")
        pv_done, o_na_ready = sem("pv_done"), sem("o_na_ready")
        pads_ready, conv_ready, silu_ready = sem("pads_ready"), sem("conv_ready"), sem("silu_ready")
        gates_x, gates_e, gates_ready = sem("gates_x"), sem("gates_e"), sem("gates_ready")
        sq_ready, qr_ready, gq_normed = sem("sq_ready"), sem("qr_ready"), sem("gq_normed")
        zg_scaled = sem("zg_scaled")
        decay_rhs, gsum_ready, gexp_ready = sem("decay_rhs"), sem("gsum_ready"), sem("gexp_ready")
        gdn_scaled, pool_scaled = sem("gdn_scaled"), sem("pool_scaled")
        lvl_ready = sem("lvl_ready")
        state_zero, state_in, state_out = sem("state_zero"), sem("state_in"), sem("state_out")
        osq_ready, orr_ready = sem("osq_ready"), sem("orr_ready")
        og_ready, og2_ready = sem("og_ready"), sem("og2_ready")
        tok_stored = sem("tok_stored")
        logits_full, router_x, router_e = sem("logits_full"), sem("router_x"), sem("router_e")
        routed, counted = sem("routed"), sem("counted")
        y_in = [sem(f"y_in{t}") for t in range(TILES)]
        combine_a, combine_b, combine_c = map(sem, ("combine_a", "combine_b", "combine_c"))
        out_stored = sem("out_stored")

        def expert_sems(tag):
            names = ("step",
                     "sel", "list_full", "list_taken",
                     "idx_copied", "gathering",
                     "transposed", "xT",
                     "a_full", "b_full", "silu", "h",
                     "hTp", "hT", "y_full", "y")
            s = {k: sem(f"{tag}_{k}") for k in names}
            s["gathered"] = [sem(f"{tag}_gathered{b}") for b in range(2)]
            s["y_stored"] = [sem(f"{tag}_y_stored{b}") for b in range(2)]
            return s

        es = expert_sems("moe")
        spare = [expert_sems(f"over{l}") for l in range(DEPTH)]
        spare_in = [[sem(f"over{l}_in{i}") for i in range(6)] for l in range(DEPTH)]

        def slot(s):
            return ring[:, s, :] if s < PRE_SLOTS else slot5

        def wide(s):
            return slot(s).rearrange("p (k n) -> p k n", k=KC)

        PRE = pre_slabs()
        pre_slot, pre_turn, held = {}, {}, [0] * PRE_SLOTS
        for slabs in PRE:
            for i, name in enumerate(slabs):
                pre_slot[name] = (i - len(slabs) + 1) % PRE_SLOTS
                held[pre_slot[name]] += 1
                pre_turn[name] = held[pre_slot[name]]

        def arrived(eng, *name):
            eng.wait_ge(slab_in[pre_slot[name]], 16 * pre_turn[name])

        slab_job = {}
        job = {}
        block = ctx.enter_context(nc.Block())

        @block.tensor
        def _(pe):
            n = Counts()
            jobs = {"dve": 0, "act": 0, "ada": 0}

            def dve_bank(*name):
                b = jobs["dve"]
                jobs["dve"] += 1
                job[name] = b + 1
                if b >= 3:
                    pe.wait_ge(dve_emptied, b - 2)
                return bank[b % 3]

            def act_bank(*name):
                b = jobs["act"]
                jobs["act"] += 1
                job[name] = b + 1
                if b >= 3:
                    pe.wait_ge(act_emptied, b - 2)
                return bank[4 + b % 3]

            def mm(out, lhsT, rhs, start=True, stop=True):
                return nc.tensor.matmul(out, lhsT, rhs, start=start, stop=stop)

            def tr(out, src, rows_=P):
                return nc.tensor.transpose(out, src, ident[0:rows_, 0:rows_])

            def tr4(b, src):
                for q in range(4):
                    last = tr(b[:, q * P:(q + 1) * P], src[:, q * P:(q + 1) * P])
                return last

            pe.wait_ge(consts_in, 16)
            pe.wait_ge(rows_in, 96)
            b = dve_bank("cols")
            tr(b[:, 0:P], rows[:, 0, :])
            tr(b[:, P:P + 120], rows[0:120, 1, :], 120)
            tr(b[:, 256:272], rows[0:16, 2, :], 16).then_inc(for_dve, 1)
            pe.wait_ge(silu_c_ready, 1)

            def ada_product(slab, k):
                if k == 0:
                    arrived(pe, *slab)
                    if jobs["ada"]:
                        pe.wait_ge(ada_taken, jobs["ada"])
                last = mm(bank[3][0:2, :], silu_c[:, k:16:8], wide(pre_slot[slab])[:, k, :], k == 0, k == KC - 1)
                if k == KC - 1:
                    last.then_inc(ada_full, 1)
                    jobs["ada"] += 1
                    slab_job[slab] = ("ada", jobs["ada"])

            def ada_cols(slab):
                no = slab_job[slab][1]
                pe.wait_ge(ada_taken, no)
                b = dve_bank("mod_col", *slab)
                for q in range(4):
                    last = tr(b[:, 2 * q:2 * q + 2], mrow[:, (no - 1) % 2, q * P:(q + 1) * P], 2)
                last.then_inc(for_dve, 1)

            for i in range(EARLY):
                for k in range(KC):
                    ada_product(("ada", 0, i), k)
                if i:
                    ada_cols(("ada", 0, i - 1))
            ada_cols(("ada", 0, EARLY - 1))
            for l in range(DEPTH):
                plan = mixing_plan([name for name in PRE[l][EARLY if l == 0 else 0:] if name[0] == "ada"])

                def point(p):
                    products, _, cols_ = plan[p]
                    for slab in cols_:
                        ada_cols(slab)
                    for slab, k in products:
                        ada_product(slab, k)

                def gate_rows(which):
                    for s in range(2):
                        for half in range(2):
                            c0 = (2, 5)[which - 1] * KC + 4 * half
                            b = act_bank("gate", l, which, s, half)
                            for q in range(4):
                                last = mm(b[:, q * P:(q + 1) * P], mods[:, l, c0 + q, s:s + 1].broadcast_to([P, P]), ident)
                            last.then_inc(for_act, 1)

                def transposed_norm(which, t0=0, t1=TILES):
                    for t in range(t0, t1):
                        pe.wait_ge(scale_ready, n(scale_ready))
                        for half in range(2):
                            if half:
                                b = act_bank("norm", l, which, t, half)
                            else:
                                b = dve_bank("norm", l, which, t, half)
                            for q in range(4):
                                c0 = (4 * half + q) * P
                                last = mm(b[:, q * P:(q + 1) * P], x[:, t, c0:c0 + P], (diag1, diag2)[which - 1][:, t, :])
                            last.then_inc(for_act if half else for_dve, 1)

                def tile_in(which, t):
                    pe.wait_ge(dve_emptied, job["norm", l, which, t, 0])
                    pe.wait_ge(act_emptied, job["norm", l, which, t, 1])

                transposed_norm(1)

                def token_major(i, t):
                    w = wide(pre_slot["win", l, i])
                    b = act_bank("win", l, i, t)
                    for k in range(KC):
                        last = mm(b[:], hT[:, k, t * P:(t + 1) * P], w[:, k, :], k == 0, k == KC - 1)
                    last.then_inc(for_act, 1)
                    slab_job["win", l, i] = ("act", jobs["act"])

                for i in range(3):
                    arrived(pe, "win", l, i)
                    for t in range(TILES):
                        if i == 0:
                            tile_in(1, t)
                        token_major(i, t)
                        if i:
                            pe.wait_ge(zn_ready, n(zn_ready))
                            b = act_bank("qkT", l, i - 1, t)
                            tr4(b, (z, z_k)[i - 1][:, t, :]).then_inc(for_act, 1)
                pe.wait_ge(past_in, 32 * (l + 1))
                b = act_bank("past", l)
                tr4(b, k_past).then_inc(for_act, 1)

                def conv_cols(f):
                    pe.wait_ge(silu_ready, n(silu_ready))
                    b = act_bank("conv_back", l, f)
                    off = (0, CTX + 4, CTX + 4 + P)
                    for t in range(TILES):
                        last = tr(b[:, t * P:(t + 1) * P], conv_acc[:, f % 2, off[t]:off[t] + P])
                    last.then_inc(for_act, 1)

                for f in range(12):
                    slab = ("win", l, 3 + f // 4)
                    if f % 4 == 0:
                        arrived(pe, *slab)
                    w = wide(pre_slot[slab])
                    b = act_bank("conv", l, f)
                    for k in range(KC):
                        last = mm(b[:, 0:TOK], w[:, k, (f % 4) * P:(f % 4 + 1) * P], hT[:, k, :], k == 0, k == KC - 1)
                    last.then_inc(for_act, 1)
                    slab_job[slab] = ("act", jobs["act"])
                    if f >= 2:
                        conv_cols(f - 2)
                conv_cols(10)
                conv_cols(11)
                arrived(pe, "win", l, 6)
                for t in range(TILES):
                    token_major(6, t)
                pe.wait_ge(weights_in, 16 * N_SMALL)
                b = dve_bank("ba", l)
                for t in range(TILES):
                    for k in range(KC):
                        last = mm(b[:, t * BA:(t + 1) * BA], hT[:, k, t * P:(t + 1) * P], w_ba[:, l, k, :],
                                  k == 0, k == KC - 1)
                last.then_inc(for_dve, 1)

                units = [(t, h) for t in range(TILES) for h in range(HEADS)]

                def score(u):
                    t, h = units[u]
                    half = slice(64 * (h % 2), 64 * (h % 2) + 64)
                    keys = slice(0, P) if t == 0 else slice(P, 512)
                    b = act_bank("score", l, u)
                    last = mm(b[:, 0:keys.stop - keys.start], qT[half, h // 2, t * P:(t + 1) * P],
                              kT[half, h // 2, keys], True, t == 0)
                    if t:
                        pe.wait_ge(bias_ready, 4 * l + 2 * (t - 1) + h // 4 + 1)
                        last = mm(b[:, 0:LAT], tab("flip"), bias[:, h // 4, h % 4, :], False, True)
                    last.then_inc(for_act, 1)

                def probs_cols(u):
                    t, h = units[u]
                    pe.wait_ge(act_emptied, job["score", l, u])
                    b = act_bank("probs", l, u)
                    for q in range(1 if t == 0 else 3):
                        last = tr(b[:, q * P:(q + 1) * P], p_sb[:, u % 2, q * P:(q + 1) * P])
                    last.then_inc(for_act, 1)

                def weigh(u):
                    t, h = units[u]
                    pe.wait_ge(act_emptied, job["probs", l, u])
                    if h == 0 and (t or l):
                        pe.wait_ge(o_na_ready, 3 * l + t)
                    values = [v_sb[:, 0, :]] if t == 0 else [v_sb[:, 1, :], v_sb[:, 2, :], v_past]
                    for q, v in enumerate(values):
                        last = mm(bank[7][:, h * HD:(h + 1) * HD], pT[:, u % 2, q * P:(q + 1) * P],
                                  v[:, h * HD:(h + 1) * HD], q == 0, q == len(values) - 1)
                    last.then_inc(pv_done, 1)

                def mixed_cols(ready, src, *name):
                    pe.wait_ge(ready, n(ready))
                    tr4(act_bank(*name), src).then_inc(for_act, 1)

                pe.wait_ge(act_emptied, job["past", l])
                score(0)
                score(1)
                for u in range(len(units)):
                    probs_cols(u)
                    if u > 2 and u % 8 == 2:
                        mixed_cols(o_na_ready, o_na, "o_na", l, u // 8 - 1)
                    if u:
                        weigh(u - 1)
                    if u + 2 < len(units):
                        score(u + 2)
                    point(u)
                weigh(len(units) - 1)
                mixed_cols(o_na_ready, o_na, "o_na", l, 2)

                pe.wait_ge(gates_ready, l + 1)
                pe.wait_ge(gq_normed, 3 * l + 3)
                for step in range(3):
                    chunks = CHUNKS[step]
                    for d in range(2):
                        t = chunks[d]
                        b = dve_bank("gsum", l, step, d)
                        mm(b[:, 0:4], tab(("le", "ge")[d]), decay[:, t, 4 * d:4 * d + 4])
                        mm(b[:, 4:8], ones, decay[:, t, 4 * d:4 * d + 4]).then_inc(for_dve, 1)
                        pe.wait_ge(decay_rhs, n(decay_rhs))
                        b = act_bank("dt", l, step, d)
                        mm(b[:], tab(("gt", "lt")[d]), flat(gb[d][0])).then_inc(for_act, 1)
                    first_point = 24 + 17 * step
                    point(first_point)
                    for d in range(2):
                        t = chunks[d]
                        pe.wait_ge(gdn_scaled, n(gdn_scaled))
                        for m, src in enumerate((gb[d][2], gq[:, t, 1], gq[:, t, 0], gb[d][4])):
                            b = act_bank("gT", l, step, d, m)
                            for h in range(GH):
                                last = tr(b[:, h * P:(h + 1) * P], src[:, h, :])
                            last.then_inc(for_act, 1)
                    for d in range(2):
                        pe.wait_ge(act_emptied, job["gT", l, step, d, 3])
                        for name, rhs in (("qk", gb[d][9]), ("kk", gb[d][8])):
                            b = dve_bank(name, l, step, d)
                            for h in range(GH):
                                last = mm(b[:, h * P:(h + 1) * P], gb[d][10][:, h, :], rhs[:, h, :])
                            last.then_inc(for_dve, 1)
                    point(first_point + 1)
                    for d in range(2):
                        pe.wait_ge(lvl_ready, n(lvl_ready))
                        b = dve_bank("t0", l, step, d)
                        for h in range(GH):
                            last = tr(b[:, h * P:(h + 1) * P], gb[d][0][:, h, :])
                        last.then_inc(for_dve, 1)
                    point(first_point + 2)
                    for level in range(1, LEVELS):
                        for d in range(2):
                            pe.wait_ge(lvl_ready, n(lvl_ready))
                            if level == 1:
                                pe.wait_ge(dve_emptied, job["t0", l, step, d])
                            else:
                                pe.wait_ge(act_emptied, job["t", l, step, level - 1, d])
                            b = act_bank("at", l, step, level, d)
                            for h in range(GH):
                                last = mm(b[:, h * P:(h + 1) * P], gb[d][0][:, h, :], gb[d][2][:, h, :])
                            last.then_inc(for_act, 1)
                        point(first_point + 1 + 2 * level)
                        for d in range(2):
                            pe.wait_ge(act_emptied, job["at", l, step, level, d])
                            b = dve_bank("tu", l, step, level, d)
                            for h in range(GH):
                                last = mm(b[:, h * P:(h + 1) * P], gb[d][1][:, h, :], gb[d][4][:, h, :])
                            last.then_inc(for_dve, 1)
                        point(first_point + 2 + 2 * level)
                        for d in range(2) if level < LEVELS - 1 else ():
                            pe.wait_ge(dve_emptied, job["tu", l, step, level, d])
                            b = act_bank("t", l, step, level, d)
                            for h in range(GH):
                                last = tr(b[:, h * P:(h + 1) * P], gb[d][4][:, h, :])
                            last.then_inc(for_act, 1)
                        if (step, level) == (1, 3):
                            mixed_cols(og_ready, flat(gq[:, 0, 0]), "og", l, 0)
                    for d in range(2):
                        pe.wait_ge(dve_emptied, job["tu", l, step, LEVELS - 1, d])
                        b = act_bank("wT", l, step, d)
                        for h in range(GH):
                            last = mm(b[:, h * P:(h + 1) * P], gb[d][3][:, h, :], gb[d][4][:, h, :])
                        last.then_inc(for_act, 1)
                    if step == 2:
                        gate_rows(1)
                    point(first_point + 15)
                    for d in range(2):
                        pe.wait_ge(act_emptied, job["wT", l, step, d])
                        pe.wait_ge(pool_scaled, 6 * l + 2 * step + d + 1)
                        if step == 0:
                            pe.wait_ge(state_zero, 2 * l + d + 1)
                        elif step == 1:
                            pe.wait_ge(state_in, 32 * (l + 1))
                        else:
                            pe.wait_ge(dve_emptied, job["kv", l, 1, d])
                        b = dve_bank("vnew", l, step, d)
                        for h in range(GH):
                            mm(b[:, h * P:(h + 1) * P], gb[d][4][:, h, :], gb[d][7][:, h, :], True, False)
                            last = mm(b[:, h * P:(h + 1) * P], gb[d][8][:, h, :], state[d][:, h, :], False, True)
                        last.then_inc(for_dve, 1)
                    point(first_point + 16)
                    for d in range(2):
                        pe.wait_ge(dve_emptied, job["vnew", l, step, d])
                        b = dve_bank("o", l, step, d)
                        for h in range(GH):
                            mm(b[:, h * P:(h + 1) * P], gb[d][5][:, h, :], state[d][:, h, :], True, False)
                            last = mm(b[:, h * P:(h + 1) * P], gb[d][9][:, h, :], gb[d][0][:, h, :], False, True)
                        last.then_inc(for_dve, 1)
                        b = dve_bank("kv", l, step, d)
                        for h in range(GH):
                            last = mm(b[:, h * P:(h + 1) * P], gb[d][6][:, h, :], gb[d][0][:, h, :])
                        last.then_inc(for_dve, 1)
                gate_rows(2)
                pe.wait_ge(og_ready, 2 * l + 2)
                tr4(act_bank("og", l, 1), flat(gb[0][10])).then_inc(for_act, 1)
                pe.wait_ge(og2_ready, l + 1)
                tr4(act_bank("og", l, 2), flat(gb[1][10])).then_inc(for_act, 1)
                for j in range(N_OUT):
                    arrived(pe, "wout", l, j)
                    w = wide(pre_slot["wout", l, j])
                    for t in range(TILES):
                        if j == 0:
                            pe.wait_ge(act_emptied, job["og", l, t])
                        b = dve_bank("wout", l, j, t)
                        for k in range(KC):
                            last = mm(b[:], hT[:, k, t * P:(t + 1) * P], w[:, k, :], k == 0, k == KC - 1)
                        last.then_inc(for_dve, 1)
                    slab_job["wout", l, j] = ("dve", jobs["dve"])
                transposed_norm(2, 0, 2)
                pe.wait_ge(ada_taken, jobs["ada"])

                def logits(t):
                    tile_in(2, t)
                    for k in range(KC):
                        last = mm(bank[3][:, t * 20:(t + 1) * 20], hT[:, k, t * P:(t + 1) * P], w_rt[:, l, k, :],
                                  k == 0, k == KC - 1)
                    last.then_inc(logits_full, 1)

                logits(0)
                logits(1)
                transposed_norm(2, 2, 3)
                logits(2)
                for t in range(TILES):
                    for half in range(2):
                        b = act_bank("tok", l, t, half)
                        for q in range(4):
                            last = tr(b[:, q * P:(q + 1) * P], hT[:, 4 * half + q, t * P:(t + 1) * P])
                        last.then_inc(for_act, 1)
                pe.wait_ge(routed, l + 1)
                b = dve_bank("place", l)
                for t in range(TILES):
                    for s in range(t + 1):
                        mm(b[:, t * 16:(t + 1) * 16], tab("lt") if s == t else ones, chosen[:, s, :],
                           s == 0, s == t)
                for s in range(TILES):
                    last = mm(b[:, 48:64], ones, chosen[:, s, :], s == 0, s == TILES - 1)
                last.then_inc(for_dve, 1)

                def lists(s, first):
                    for group in range(4):
                        g = first // 4 + group
                        pe.wait_ge(s["sel"], g + 1)
                        if g >= 2:
                            pe.wait_ge(s["list_taken"], g - 1)
                        for e in range(4):
                            for t in range(TILES):
                                last = mm(bank[6 + group % 2][:, 2 * e:2 * e + 2], sel[group % 2][:, t, e, :], tokid_b[:, t, :],
                                          t == 0, t == TILES - 1)
                        last.then_inc(s["list_full"], 1)

                def run_experts(s, slab_sems, first):
                    def tokens(j, pair):
                        pe.wait_ge(s["gathered"][j], 16 * (pair + 1))
                        for half in range(2):
                            tr4(bank[half], x_e[:, j, half * 512:(half + 1) * 512]).then_inc(s["transposed"], 1)

                    def step(e, j, pair, kind=""):
                        w1, w3 = (wide(MOE_SLOTS[3 * j + m]) for m in range(2))
                        pe.wait_ge(s["xT"], e * 2 + 2)
                        if kind != "first":
                            h_cols(e - 1, 1 - j)
                        pe.wait_ge(slab_sems[3 * j], 16 * (pair + 1))
                        for k in range(KC):
                            last = mm(bank[2 + j][:], xT_e[:, j, k, :], w1[:, k, :], k == 0, k == KC - 1)
                        last.then_inc(s["a_full"], 1)
                        if kind != "first":
                            pe.wait_ge(s["hT"], e)
                        if kind != "last":
                            tokens(1 - j, pair + j)
                        pe.wait_ge(slab_sems[3 * j + 1], 16 * (pair + 1))
                        for k in range(KC):
                            last = mm(bank[4 + j][:], xT_e[:, j, k, :], w3[:, k, :], k == 0, k == KC - 1)
                        last.then_inc(s["b_full"], 1)
                        if kind != "first":
                            down(e - 1, 1 - j, pair + (j - 1), kind == "second" and first == 0)

                    def h_cols(e, j):
                        pe.wait_ge(s["h"], e + 1)
                        tr4(bank[0], h_e[:, j, :]).then_inc(s["hTp"], 1)

                    def down(e, j, pair, first_ever=False):
                        w2 = slot(MOE_SLOTS[3 * j + 2]).rearrange("p (k n) -> p k n", k=4)
                        pe.wait_ge(slab_sems[3 * j + 2], 16 * (pair + 1))
                        for half in range(2):
                            if not first_ever:
                                pe.wait_ge(s["y"], e * 2 + half - 1)
                            for k in range(4):
                                last = mm(bank[6 + half][:], hT_e[:, j, k, :], w2[:, k, half * 512:(half + 1) * 512],
                                          k == 0, k == 3)
                            last.then_inc(s["y_full"], 1)

                    pair = first // 2
                    tokens(0, pair)
                    step(first, 0, pair, "first")
                    step(first + 1, 1, pair, "second")
                    step(first + 2, 0, pair + 1)
                    with pe.Fori(2, EXPERTS // 2) as i:
                        step(i * 2 + (first - 1), 1, i + (pair - 1))
                        step(i * 2 + first, 0, i + pair)
                    step(first + EXPERTS - 1, 1, pair + EXPERTS // 2 - 1, "last")
                    h_cols(first + EXPERTS - 1, 1)
                    pe.wait_ge(s["hT"], first + EXPERTS)
                    down(first + EXPERTS - 1, 1, pair + EXPERTS // 2 - 1)
                    pe.wait_ge(s["y"], 2 * (first + EXPERTS))

                pe.wait_ge(dve_emptied, jobs["dve"])
                pe.wait_ge(act_emptied, jobs["act"])
                lists(es, l * EXPERTS)
                run_experts(es, moe_in, l * EXPERTS)
                pe.wait_ge(counted, l + 1)
                top = pe.value_load(most[0:1, 0:1])
                with pe.If(top > CAP):
                    for again in range(OVER):
                        lists(spare[l], again * EXPERTS)
                        run_experts(spare[l], spare_in[l], again * EXPERTS)

        @block.sync
        def _(sp):
            n = Counts()
            sp.dma_start(rows[0:96, 0, :], ada_b.rearrange("l (j p) -> (l j) p", p=P)).then_inc(rows_in, 16)
            sp.dma_start(rows[96:112, 0, :], norm1_g.rearrange("l (k p) -> (l k) p", p=P)).then_inc(rows_in, 16)
            sp.dma_start(rows[112:128, 0, :], norm2_g.rearrange("l (k p) -> (l k) p", p=P)).then_inc(rows_in, 16)
            sp.dma_start(rows[0:120, 1, :], gdn_conv_w.rearrange("l t (f p) -> (l t f) p", p=P)).then_inc(rows_in, 16)
            sp.dma_start(rows[0:8, 2, :], c_ctx.rearrange("(k p) -> k p", p=P)).then_inc(rows_in, 16)
            sp.dma_start(rows[8:16, 2, :], c.rearrange("b (k p) -> (b k) p", p=P)).then_inc(rows_in, 16)
            sp.dma_start(const[:], tables).then_inc(consts_in, 16)

            def expert_slabs(i, l):
                for j in range(2):
                    e = l * EXPERTS + 2 * i + j
                    yield moe_w1.rearrange("l e (k p) n -> p (l e) k n", p=P)[:, bass.ds(e, 1)]
                    yield moe_w3.rearrange("l e (k p) n -> p (l e) k n", p=P)[:, bass.ds(e, 1)]
                    yield moe_w2.rearrange("l e (k p) n -> p (l e) k n", p=P)[:, bass.ds(e, 1)]

            def put(s, src, done):
                dst = slot(s).rearrange("p (o k n) -> p o k n", o=1, k=src.shape[2])
                sp.dma_start(dst, src).then_inc(done, 16)

            def slab_done(name):
                who, no = slab_job[name]
                sp.wait_ge({"dve": for_dve, "act": for_act, "ada": ada_full}[who], no)

            def moe_done(s, m, e):
                e = e + m // 3
                if m % 3 == 2:
                    sp.wait_ge(s["y_full"], e * 2 + 2)
                else:
                    sp.wait_ge(s["a_full"] if m % 3 == 0 else s["b_full"], e + 1)

            def store_y(s, e, rel, j, offset):
                sp.wait_ge(s["y"], e * 2 + 2)
                dst = expert_dram.rearrange("(e r) n -> r e n", r=CAP)[:, bass.ds(rel + offset * EXPERTS, 1)]
                sp.dma_start(dst, y_e[0:CAP, j, :].unsqueeze(1)).then_inc(s["y_stored"][j], 16)

            for l in range(DEPTH):
                for i, name in enumerate(PRE[l]):
                    if l and i == 0:
                        sp.wait_ge(y_in[TILES - 1], 32 * l)
                    s = pre_slot[name]
                    if i >= PRE_SLOTS:
                        slab_done(PRE[l][i - PRE_SLOTS])
                    elif l:
                        moe_done(es, MOE_SLOTS.index(s), l * EXPERTS - 2)
                    kind, layer, j = name
                    weights = {"ada": ada_w, "win": w_in, "wout": w_out}[kind]
                    if (l, i) == (0, EARLY):
                        sp.dma_start(x[:, 0, :], x_prompt[0]).then_inc(x_in, 16)
                        sp.dma_start(x[:, 1:3, :], x_sample.rearrange("b (t p) n -> p (b t) n", p=P)).then_inc(x_in, 16)
                    src = weights[layer].rearrange("(k p) n -> p k n", p=P)[:, :, j * 512:(j + 1) * 512]
                    sp.dma_start(wide(s), src).then_inc(slab_in[s], 16)
                for m, src in enumerate(expert_slabs(0, l)):
                    s = MOE_SLOTS[m]
                    if s == 5:
                        sp.wait_ge(for_act, job["og", l, 2])
                    else:
                        slab_done([name for name in PRE[l] if pre_slot[name] == s][-1])
                    put(s, src, moe_in[m])
                with sp.Fori(1, EXPERTS // 2) as i:
                    for m, src in enumerate(expert_slabs(i, l)):
                        moe_done(es, m, i * 2 + (l * EXPERTS - 2))
                        put(MOE_SLOTS[m], src, moe_in[m])
                        if m % 3 == 2:
                            j = m // 3
                            store_y(es, i * 2 + (l * EXPERTS - 2 + j), i * 2 + (j - 2), j, 0)
                for j in range(2):
                    store_y(es, (l + 1) * EXPERTS - 2 + j, EXPERTS - 2 + j, j, 0)
                sp.wait_ge(counted, l + 1)
                top = sp.value_load(most[0:1, 0:1])
                with sp.If(top > CAP):
                    for again in range(OVER):
                        for m, src in enumerate(expert_slabs(0, l)):
                            if again:
                                moe_done(spare[l], m, again * EXPERTS - 2)
                            else:
                                moe_done(es, m, (l + 1) * EXPERTS - 2)
                            put(MOE_SLOTS[m], src, spare_in[l][m])
                        with sp.Fori(1, EXPERTS // 2) as i:
                            for m, src in enumerate(expert_slabs(i, l)):
                                moe_done(spare[l], m, i * 2 + (again * EXPERTS - 2))
                                put(MOE_SLOTS[m], src, spare_in[l][m])
                                if m % 3 == 2:
                                    j = m // 3
                                    store_y(spare[l], i * 2 + (again * EXPERTS - 2 + j), i * 2 + (j - 2), j,
                                            again + 1)
                        for j in range(2):
                            store_y(spare[l], (again + 1) * EXPERTS - 2 + j, EXPERTS - 2 + j, j, again + 1)
                    for m in range(6):
                        moe_done(spare[l], m, OVER * EXPERTS - 2)
            for t in range(TILES):
                sp.wait_ge(x_ready, TILES * (2 * DEPTH - 1) + t + 1)
                dst = y_prompt[0] if t == 0 else y_sample[0, (t - 1) * P:t * P]
                sp.dma_start(dst, x[:, t, :]).then_inc(out_stored, 16)
            sp.wait_ge(out_stored, 16 * TILES)
            sp.wait_ge(kv_stored, 32 * DEPTH)
            sp.wait_ge(state_out, 32 * DEPTH)
            for b in range(2):
                sp.wait_ge(es["y_stored"][b], 16 * DEPTH * EXPERTS // 2)

        @block.scalar
        def _(act):
            n = Counts()

            def filled(*name):
                act.wait_ge(for_act, job[name])
                return bank[4 + (job[name] - 1) % 3]

            def link(ins):
                ins.then_inc(act_step, 1)
                act.wait_ge(act_step, n(act_step))

            def f(out, in_, func=ACT.Copy, **kw):
                return nc.scalar.activation(out, in_, func, **kw)

            act.wait_ge(consts_in, 16)
            one = ones[:, 0:1]
            act.wait_ge(dve_emptied, job["cols",])
            f(silu_c[:], cols[:, 2, 0:16], ACT.Exp, scale=-1.0).then_inc(c_exp, 1)
            arrived(act, "ada", 0, 0)
            for l in range(DEPTH):
                act.dma_start(w_ba[:, l], w_in[l].rearrange("(k p) n -> p k n", p=P)[:, :, N_IN - BA:N_IN]).then_inc(weights_in, 16)
                act.dma_start(w_rt[:, l, :, 0:4], moe_w_rg[l].rearrange("(k p) n -> p k n", p=P)).then_inc(weights_in, 16)
                act.dma_start(w_rt[:, l, :, 4:20], moe_w_re[l].rearrange("(k p) n -> p k n", p=P)).then_inc(weights_in, 16)
            for dst, src in (
                    (b_rt[:, :, 0:4], moe_b_rg), (b_rt[:, :, 4:20], moe_b_re),
                    (head_g[:, :, 0, :], na_qn_g), (head_g[:, :, 1, :], na_kn_g), (gdn_g[:], gdn_norm_g),
                    (gate_c[:, :, 0, :], gdn_a_log.rearrange("l d h -> l (d h)")),
                    (gate_c[:, :, 1, :], gdn_dt_bias.rearrange("l d h -> l (d h)"))):
                act.dma_start(dst, src.unsqueeze(0).broadcast_to([P] + list(src.shape))).then_inc(weights_in, 16)

            def squares(l, which, t, half):
                if n.seen.get(ss_ready.name):
                    act.wait_ge(ss_ready, n.seen[ss_ready.name])
                n(ss_ready)
                f((junk1, junk2)[which - 1], x[:, t, half * 512:(half + 1) * 512], ACT.Square,
                  accum_out=ss[:, t, half:half + 1]).then_inc(ss_ready, 1)

            def modulated(l, which, t):
                shift, scale = ((0, 1), (3, 4))[which - 1]
                b = filled("norm", l, which, t, 1)
                for q in range(4):
                    k, s = 4 + q, STREAM[t]
                    last = f(hT[:, k, t * P:(t + 1) * P], b[:, q * P:(q + 1) * P], ACT.Identity,
                             scale=mods[:, l, scale * KC + k, s:s + 1], bias=mods[:, l, shift * KC + k, s:s + 1])
                last.then_inc(act_emptied, 1)

            def gate_rows(l, which):
                for s in range(2):
                    dst = gate1[s] if which == 1 else gate2[:, s, :]
                    for half in range(2):
                        b = filled("gate", l, which, s, half)
                        f(dst[:, half * 512:(half + 1) * 512], b[:]).then_inc(act_emptied, 1)

            for l in range(DEPTH):
                for t in range(TILES):
                    if l:
                        act.wait_ge(x_ready, 6 * l - 2 + t)
                    elif t == 0:
                        act.wait_ge(x_in, 32)
                    for half in range(2):
                        squares(l, 1, t, half)
                for t in range(TILES):
                    modulated(l, 1, t)

                def token_tile(which, t):
                    b = filled("win", l, which, t)
                    j = 3 * which + t
                    if which == 2:
                        f(v_sb[:, t, :], b[:]).then_inc(act_emptied, 1)
                        return
                    f((z, z_k)[which][:, t, :], b[:])
                    if j >= 2:
                        act.wait_ge(zn_ready, 6 * l + j - 1)
                    f(sq[:, j % 2, :], b[:], ACT.Square).then_inc(act_emptied, 1)

                def qk_cols(which, t):
                    b = filled("qkT", l, which, t)
                    dst = (qT, kT)[which]
                    f(dst[:, :, t * P:(t + 1) * P], b[:].rearrange("p (h n) -> p h n", h=4)).then_inc(act_emptied, 1)

                def bias_lot(lot):
                    t, h4 = 1 + lot // 2, lot % 2
                    for row in range(2):
                        q_row = 2 * (t - 1) + row
                        for h in range(4):
                            at = ((l * HEADS + 4 * h4 + h) * RPB_H + 7 - q_row) * RPB_W + NA_KW - GRID_W
                            src = bass.AP(na_rpb.tensor, at, [[1, GRID_W], [RPB_W, ROWS], [1, GRID_W]])
                            dst = bias[row * GRID_W:(row + 1) * GRID_W, h4, h, :].rearrange("p (r n) -> p r n", r=ROWS)
                            act.dma_start(dst, src).then_inc(bias_in[h4], 16)

                for which in range(3):
                    for t in range(TILES):
                        j = 3 * which + t
                        token_tile(which, t)
                        if which:
                            qk_cols(which - 1, t)
                act.wait_ge(kv_stored, 32 * (l + 1))
                bias_lot(0)
                bias_lot(1)
                b = filled("past", l)
                f(kT[:, :, TOK:512], b[:].rearrange("p (h n) -> p h n", h=4)).then_inc(act_emptied, 1)

                act.wait_ge(pads_ready, l + 1)

                def conv_silu(c):
                    act.wait_ge(conv_ready, 12 * l + c + 1)
                    f(conv_acc[:, c % 2, :], conv_acc[:, c % 2, :], ACT.Silu).then_inc(silu_ready, 1)

                def conv_back(c):
                    b = filled("conv_back", l, c)
                    f(gq[:, :, c // 4, c % 4, :], b[:, 0:TOK].rearrange("p (t n) -> p t n", t=TILES)).then_inc(act_emptied, 1)

                for c in range(12):
                    b = filled("conv", l, c)
                    if c >= 2:
                        act.wait_ge(conv_ready, 12 * l + c - 1)
                    f(conv_in[:, c % 2, 2:2 + CTX], b[:, 0:CTX])
                    f(conv_in[:, c % 2, CTX + 6:CTX + 6 + LAT], b[:, CTX:TOK]).then_inc(act_emptied, 1)
                    if c >= 2:
                        conv_back(c - 2)
                    if c:
                        conv_silu(c - 1)
                conv_back(10)
                conv_silu(11)
                conv_back(11)
                for t in range(TILES):
                    b = filled("win", l, 6, t)
                    f(zg[:, t, :], b[:], ACT.Silu).then_inc(act_emptied, 1)
                def probs(u):
                    t, h = divmod(u, HEADS)
                    keys = CTX if t == 0 else LAT + PAST
                    b = filled("score", l, u)
                    act.wait_ge(s_ready, 24 * l + u + 1)
                    f(p_sb[:, u % 2, 0:keys], b[:, 0:keys], ACT.Exp, bias=neg_max[:, t, h:h + 1],
                      accum_out=row_sum[:, t, h:h + 1]).then_inc(act_emptied, 1)

                def probs_T(u):
                    keys = CTX if u < HEADS else LAT + PAST
                    b = filled("probs", l, u)
                    if l or u >= 2:
                        act.wait_ge(pv_done, 24 * l + u - 1)
                    f(pT[:, u % 2, 0:keys], b[:, 0:keys]).then_inc(act_emptied, 1)

                def mixed_T(name, t, k0):
                    b = filled(name, l, t)
                    f(hT[:, k0:k0 + 4, t * P:(t + 1) * P], b[:].rearrange("p (k n) -> p k n", k=4)).then_inc(act_emptied, 1)

                probs(0)
                for u in range(TILES * HEADS):
                    if u + 1 < TILES * HEADS:
                        probs(u + 1)
                    probs_T(u)
                    if u == 3:
                        act.wait_ge(gates_x, l + 1)
                        link(f(gabs, gabs, ACT.Exp, scale=-1.0))
                        f(gabs, gabs, ACT.Ln, bias=one)
                        f(beta, ba[:, :, 0:8], ACT.Exp, scale=-1.0)
                        f(ea, gate_c[:, l, 0, :], ACT.Exp).then_inc(gates_e, 1)
                    if u in (10, 14):
                        bias_lot(2 + (u - 10) // 4)
                    if u > 2 and u % 8 == 2:
                        mixed_T("o_na", u // 8 - 1, 0)
                mixed_T("o_na", 2, 0)

                for step in range(3):
                    for d in range(2):
                        b = filled("dt", l, step, d)
                        f(flat(gb[d][1]), b[:], ACT.Exp).then_inc(act_emptied, 1)
                        act.wait_ge(gsum_ready, n(gsum_ready))
                        f(gexp[d], gsum[d], ACT.Exp).then_inc(gexp_ready, 1)
                    for d in range(2):
                        for m, dst in enumerate((8, 10, 9, 5)):
                            b = filled("gT", l, step, d, m)
                            f(flat(gb[d][dst]), b[:]).then_inc(act_emptied, 1)
                    for level in range(1, LEVELS):
                        for d in range(2):
                            b = filled("at", l, step, level, d)
                            f(flat(gb[d][1]), b[:]).then_inc(act_emptied, 1)
                        for d in range(2) if level < LEVELS - 1 else ():
                            b = filled("t", l, step, level, d)
                            f(flat(gb[d][2]), b[:]).then_inc(act_emptied, 1)
                        if (step, level) == (1, 2):
                            act.wait_ge(state_out, 32 * (l + 1))
                            for d in range(2):
                                act.dma_start(state[d], state_ssm[0, l, d].rearrange("h k v -> k h v")).then_inc(state_in, 16)
                        if (step, level) == (1, 3):
                            mixed_T("og", 0, 4)
                    for d in range(2):
                        b = filled("wT", l, step, d)
                        f(flat(gb[d][8]), b[:]).then_inc(act_emptied, 1)
                    if step == 2:
                        gate_rows(l, 1)
                    for t in OUTS[step]:
                        act.wait_ge(dve_emptied, job["o", l, step, t % 2 if step else 1])
                        if step and t == 1:
                            act.wait_ge(osq_ready, 3 * l + 2)
                        for h in range(GH):
                            last = f(gq[:, 0, 1, h, :], o_acc[:, max(t - 1, 0), h * P:(h + 1) * P], ACT.Square,
                                     accum_out=oss[:, t, h:h + 1])
                        last.then_inc(osq_ready, 1)
                    if step == 0:
                        for d in range(2):
                            act.wait_ge(dve_emptied, job["kv", l, 0, d])
                            act.dma_start(new_state[0, l, d].rearrange("h k v -> k h v"), state[d]).then_inc(state_out, 16)
                gate_rows(l, 2)
                for t in (1, 2):
                    mixed_T("og", t, 4)

                for half in range(2):
                    for t in range(TILES):
                        if half:
                            act.wait_ge(x_ready, 6 * l + t + 1)
                        else:
                            act.wait_ge(x_half, 3 * l + t + 1)
                        squares(l, 2, t, half)
                modulated(l, 2, 0)
                modulated(l, 2, 1)
                modulated(l, 2, 2)
                for t in range(TILES):
                    for half in range(2):
                        b = filled("tok", l, t, half)
                        f(tok_sb[:, t, half * 512:(half + 1) * 512], b[:]).then_inc(act_emptied, 1)
                act.wait_ge(router_x, l + 1)
                f(r_exp, r_exp, ACT.Exp).then_inc(router_e, 1)

                def run_experts(s, first):
                    def tokens_T(e, j, first_ever=False):
                        for half in range(2):
                            act.wait_ge(s["transposed"], e * 2 + half + 1)
                            if not first_ever:
                                act.wait_ge(s["b_full"], e - 1)
                            f(xT_e[:, j, 4 * half:4 * half + 4, :],
                              bank[half][:].rearrange("p (k n) -> p k n", k=4)).then_inc(s["xT"], 1)

                    def silu(e, j, first_ever=False):
                        act.wait_ge(s["a_full"], e + 1)
                        if not first_ever:
                            act.wait_ge(s["h"], e - 1)
                        f(silu_a[:, j, :], bank[2 + j][:], ACT.Silu).then_inc(s["silu"], 1)

                    def h_T(e, j):
                        act.wait_ge(s["hTp"], e + 1)
                        f(hT_e[:, j, :, :], bank[0][:].rearrange("p (k n) -> p k n", k=4)).then_inc(s["hT"], 1)

                    def step(e, j, first_ever=False):
                        h_T(e - 1, 1 - j)
                        silu(e, j, first_ever)
                        tokens_T(e + 1, 1 - j)

                    tokens_T(first, 0, first == 0)
                    silu(first, 0, first == 0)
                    tokens_T(first + 1, 1, first == 0)
                    step(first + 1, 1, first == 0)
                    step(first + 2, 0)
                    with act.Fori(2, EXPERTS // 2) as i:
                        step(i * 2 + (first - 1), 1)
                        step(i * 2 + first, 0)
                    h_T(first + EXPERTS - 2, 0)
                    silu(first + EXPERTS - 1, 1)
                    h_T(first + EXPERTS - 1, 1)

                run_experts(es, l * EXPERTS)
                act.wait_ge(counted, l + 1)
                top = act.value_load(most[0:1, 0:1])
                with act.If(top > CAP):
                    for again in range(OVER):
                        run_experts(spare[l], again * EXPERTS)

                for t in range(TILES):
                    act.wait_ge(y_in[t], 32 * (l + 1))
                    f(y_first[:, t, :], y_first[:, t, :], scale=w_tok[:, t, 0:1]).then_inc(combine_a, 1)

        @block.vector
        def _(dve):
            n = Counts()
            vec = nc.vector
            last_job = [0]

            def filled(*name):
                assert job[name] == last_job[0] + 1, name
                last_job[0] += 1
                dve.wait_ge(for_dve, job[name])
                return bank[(job[name] - 1) % 3]

            def link(ins):
                ins.then_inc(dve_step, 1)
                dve.wait_ge(dve_step, n(dve_step))

            def tt(out, a, b, op=ALU.mult):
                return vec.tensor_tensor(out, a, b, op)

            def ts(out, a, s1, s2=None, op0=ALU.mult, op1=None):
                if op1 is None:
                    return vec.tensor_scalar(out, a, s1, None, op0)
                return vec.tensor_scalar(out, a, s1, s2, op0, op1)

            def stt(out, a, s, b, op0, op1):
                return vec.scalar_tensor_tensor(out, a, s, b, op0, op1)

            b = filled("cols")
            vec.tensor_copy(cols[:, 0, :], b[:, 0:P])
            vec.tensor_copy(cols[:, 1, 0:120], b[:, P:P + 120])
            vec.tensor_copy(cols[:, 2, 0:16], b[:, 256:272]).then_inc(dve_emptied, 1)
            dve.wait_ge(consts_in, 16)
            vec.tensor_copy(tokid_b[:], tab("tokid"))
            dve.wait_ge(c_exp, 1)
            link(ts(silu_c[:], silu_c[:], 1.0, op0=ALU.add))
            link(vec.reciprocal(silu_c[:], silu_c[:]))
            tt(silu_c[:], silu_c[:], cols[:, 2, 0:16]).then_inc(silu_c_ready, 1)
            def inverse_root(dst, src, scale, done=None):
                m = dst.shape[1]
                v, y, t = nv[:, 0:m], ny[:, 0:m], nt[:, 0:m]
                link(ts(v, src, scale, EPS, ALU.mult, ALU.add))
                link(ts(y.bitcast(I32), v.bitcast(I32), 1, op0=ALU.logical_shift_right))
                link(ts(y.bitcast(I32), y.bitcast(I32), -1.0, float(0x5f3759df), ALU.mult, ALU.add))
                for step in range(3):
                    link(tt(t, y, y))
                    link(stt(t, t, -0.5, v, ALU.mult, ALU.mult))
                    ins = stt(dst if step == 2 else y, t, 1.5, y, ALU.add, ALU.mult)
                    if step == 2 and done:
                        ins.then_inc(done, 1)
                        dve.wait_ge(done, n(done))
                    else:
                        link(ins)

            def token_scales(l, which, t0, t1):
                dve.wait_ge(ss_ready, 12 * l + 6 if which == 1 else 12 * l + 9 + t1)
                link(tt(ssum[:, t0:t1], ss[:, t0:t1, 0], ss[:, t0:t1, 1], ALU.add))
                inverse_root(rstd[:, t0:t1], ssum[:, t0:t1], 1.0 / D)
                for t in range(t0, t1):
                    ts((diag1, diag2)[which - 1][:, t, :], ident, rstd[:, t:t + 1]).then_inc(scale_ready, 1)

            def ada_row(slab):
                no = slab_job[slab][1]
                dve.wait_ge(ada_full, no)
                vec.tensor_copy(mrow[:, (no - 1) % 2, :], bank[3][0:2, :]).then_inc(ada_taken, 1)

            def ada_col(slab):
                _, layer, i = slab
                b = filled("mod_col", *slab)
                tt(mods[:, layer, 4 * i:4 * i + 4, :], b[:, 0:8].rearrange("p (q s) -> p q s", s=2),
                   over(cols[:, 0, 48 * layer + 4 * i:48 * layer + 4 * i + 4], 2), ALU.add).then_inc(dve_emptied, 1)
                if i in (3, 9):
                    dve.wait_ge(dve_emptied, job[("mod_col", *slab)])
                    m, g0 = (1, 96) if i == 3 else (4, 112)
                    part = mods[:, layer, m * KC:(m + 1) * KC, :]
                    link(stt(part, part, 1.0, over(cols[:, 0, g0 + KC * layer:g0 + KC * layer + KC], 2),
                             ALU.add, ALU.mult))

            for i in range(EARLY):
                ada_row(("ada", 0, i))
                if i:
                    ada_col(("ada", 0, i - 1))
            ada_col(("ada", 0, EARLY - 1))
            for l in range(DEPTH):
                mod = mods[:, l]
                plan = mixing_plan([name for name in PRE[l][EARLY if l == 0 else 0:] if name[0] == "ada"])

                def point(p):
                    _, rows_, cols_ = plan[p]
                    for slab in cols_:
                        ada_col(slab)
                    for slab in rows_:
                        ada_row(slab)

                def modulated(which):
                    shift, scale = ((0, 1), (3, 4))[which - 1]
                    for t in range(TILES):
                        s = STREAM[t]
                        b = filled("norm", l, which, t, 0)
                        for k in range(4):
                            last = ts(hT[:, k, t * P:(t + 1) * P], b[:, k * P:(k + 1) * P],
                                      mod[:, scale * KC + k, s:s + 1], mod[:, shift * KC + k, s:s + 1],
                                      ALU.mult, ALU.add)
                        last.then_inc(dve_emptied, 1)

                token_scales(l, 1, 0, TILES)
                modulated(1)
                if l == 0:
                    dve.wait_ge(weights_in, 16 * N_SMALL)
                for j in range(6):
                    which, t = divmod(j, 3)
                    dst = (z, z_k)[which][:, t, :]
                    dst3 = dst.rearrange("p (h n) -> p h n", h=HEADS)
                    dve.wait_ge(act_emptied, job["win", l, which, t])
                    link(vec.reduce_sum(hss[:, j % 2, :], sq[:, j % 2, :].rearrange("p (h n) -> p h n", h=HEADS), AX))
                    inverse_root(hr[:, j % 2, :], hss[:, j % 2, :], 1.0 / HD)
                    link(tt(dst3, dst3, over(hr[:, j % 2, :], HD)))
                    stt(dst3, dst3, (HD ** -0.5, 1.0)[which], heads(head_g[:, l, which, :], HEADS),
                        ALU.mult, ALU.mult).then_inc(zn_ready, 1)

                for c in range(12):
                    acc, src = conv_acc[:, c % 2, :], conv_in[:, c % 2, :]
                    dve.wait_ge(act_emptied, job["conv", l, c])
                    if c >= 2:
                        dve.wait_ge(for_act, job["conv_back", l, c - 2])
                    for tap in range(CONV):
                        w = cols[:, 1, 60 * l + 12 * tap + c:60 * l + 12 * tap + c + 1]
                        if tap == 0:
                            link(ts(acc, src[:, 0:CO], w))
                        elif tap < CONV - 1:
                            link(stt(acc, src[:, tap:tap + CO], w, acc, ALU.mult, ALU.add))
                        else:
                            stt(acc, src[:, tap:tap + CO], w, acc, ALU.mult, ALU.add).then_inc(conv_ready, 1)
                b = filled("ba", l)
                vec.tensor_copy(ba, b[:, 0:48].rearrange("p (t n) -> p t n", t=TILES)).then_inc(dve_emptied, 1)
                dve.wait_ge(dve_emptied, job["ba", l])
                link(tt(ga, ba[:, :, 8:16], heads(gate_c[:, l, 1, :], TILES), ALU.add))
                stt(gabs, ga, -1.0, ga, ALU.mult, ALU.max).then_inc(gates_x, 1)
                def maxima(u):
                    t, h = divmod(u, HEADS)
                    keys = CTX if t == 0 else LAT + PAST
                    dve.wait_ge(for_act, job["score", l, u])
                    b = bank[4 + (job["score", l, u] - 1) % 3]
                    vec.tensor_reduce(neg_max[:, t, h:h + 1], b[:, 0:keys], AX, ALU.max, negate=True).then_inc(s_ready, 1)

                def outputs(t):
                    dve.wait_ge(pv_done, 24 * l + 8 * (t + 1))
                    if t:
                        dve.wait_ge(for_act, job["o_na", l, t - 1])
                    link(vec.reciprocal(row_sum[:, t, :], row_sum[:, t, :]))
                    tt(o_na.rearrange("p (h n) -> p h n", h=HEADS), bank[7][:].rearrange("p (h n) -> p h n", h=HEADS),
                       over(row_sum[:, t, :], HD)).then_inc(o_na_ready, 1)

                for u in range(TILES * HEADS):
                    maxima(u)
                    if u >= 2:
                        point(u - 2)
                    if u > 8 and u % 8 == 1:
                        outputs(u // 8 - 1)
                    if u == 6:
                        link(ts(ga, ga, 0.0, op0=ALU.max))
                        dve.wait_ge(gates_e, l + 1)
                        link(tt(ga, ga, gabs, ALU.add))
                        link(stt(decay, ga, -1.0, heads(ea, TILES), ALU.mult, ALU.mult))
                        link(ts(beta, beta, 1.0, op0=ALU.add))
                        vec.reciprocal(beta, beta).then_inc(gates_ready, 1)
                    if u in NORM_AT:
                        t = NORM_AT.index(u)
                        dve.wait_ge(sq_ready, 3 * l + t + 1)
                        link(vec.reduce_sum(qss[:, t, :], sq8, AX))
                        inverse_root(qr[:, t, :], qss[:, t, :], 1.0)
                        ts(qr[:, t, 0:4], qr[:, t, 0:4], GD ** -0.5).then_inc(qr_ready, 1)
                point(22)
                point(23)
                outputs(2)

                def gated(t, dst):
                    acc = o_acc[:, max(t - 1, 0), :]
                    acc3 = acc.rearrange("p (h n) -> p h n", h=GH)
                    link(tt(acc3, acc3, over(orr[:, t, :], GD)))
                    tt(dst, acc, zg[:, t, :]).then_inc(og_ready, 1)

                def gated_output(t, dst):
                    dve.wait_ge(osq_ready, 3 * l + t + 1)
                    dve.wait_ge(zg_scaled, 3 * l + 3)
                    inverse_root(orr[:, t, :], oss[:, t, :], 1.0 / GD)
                    gated(t, dst)

                incl = [tab("le"), tab("ge")]
                dve.wait_ge(for_act, job["o_na", l, 2])
                dve.wait_ge(gates_ready, l + 1)
                dve.wait_ge(gq_normed, 3 * l + 3)
                for step in range(3):
                    for d in range(2):
                        b = filled("gsum", l, step, d)
                        vec.tensor_copy(gsum[d][:, 0:8], b[:, 0:8]).then_inc(dve_emptied, 1)
                        dve.wait_ge(dve_emptied, job["gsum", l, step, d])
                        tt(gsum[d][:, 8:12], gsum[d][:, 4:8], gsum[d][:, 0:4], ALU.subtract).then_inc(gsum_ready, 1)
                    first_point = 24 + 17 * step
                    point(first_point)
                    for d in range(2):
                        t = CHUNKS[step][d]
                        q_, k_ = gq[:, t, 0], gq[:, t, 1]
                        bt = over(beta[:, t, 4 * d:4 * d + 4], GD)
                        dve.wait_ge(gexp_ready, 6 * l + 2 * step + d + 1)
                        tt(gb[d][4], q_, over(gexp[d][:, 0:4], GD))
                        link(tt(gb[d][2], k_, bt))
                        stt(gb[d][3], gb[d][2], -1.0, over(gexp[d][:, 0:4], GD), ALU.mult, ALU.mult).then_inc(gdn_scaled, 1)
                        dve.wait_ge(act_emptied, job["dt", l, step, d])
                        link(tt(gb[d][1], gb[d][1], heads(incl[d], GH)))
                    for d in range(2):
                        for name, dst in (("qk", 9), ("kk", 10)):
                            b = filled(name, l, step, d)
                            tt(gb[d][dst], b[:].rearrange("p (h n) -> p h n", h=GH), gb[d][1]).then_inc(dve_emptied, 1)
                    point(first_point + 1)
                    for d in range(2):
                        dve.wait_ge(lvl_ready, 42 * l + 14 * step + d + 1)
                        tt(gb[d][4], heads(ident, GH), gb[d][0], ALU.subtract)
                        b = filled("t0", l, step, d)
                        tt(gb[d][2], heads(ident, GH), b[:].rearrange("p (h n) -> p h n", h=GH),
                           ALU.subtract).then_inc(dve_emptied, 1)
                    point(first_point + 2)
                    for level in range(1, LEVELS):
                        point(first_point + 1 + 2 * level)
                        for d in range(2):
                            if level == 1:
                                dve.wait_ge(dve_emptied, job["t0", l, step, d])
                            else:
                                dve.wait_ge(dve_emptied, job["tu", l, step, level - 1, d])
                            b = filled("tu", l, step, level, d)
                            tt(gb[d][4], gb[d][4], b[:].rearrange("p (h n) -> p h n", h=GH),
                               ALU.subtract).then_inc(dve_emptied, 1)
                        point(first_point + 2 + 2 * level)
                        if (step, level) == (1, 1):
                            gated_output(0, flat(gq[:, 0, 0]))
                    point(first_point + 15)
                    for d in range(2):
                        b = filled("vnew", l, step, d)
                        vec.tensor_copy(flat(gb[d][0]), b[:]).then_inc(dve_emptied, 1)
                    point(first_point + 16)
                    for d in range(2):
                        t = CHUNKS[step][d]
                        acc = o_acc[:, max(t - 1, 0), :]
                        b = filled("o", l, step, d)
                        if (step, d) in ((0, 0), (1, 0), (1, 1)):
                            vec.tensor_copy(acc, b[:]).then_inc(dve_emptied, 1)
                        else:
                            dve.wait_ge(dve_emptied, job["o", l, step, d] - 1)
                            tt(acc, acc, b[:], ALU.add).then_inc(dve_emptied, 1)
                        b = filled("kv", l, step, d)
                        for h in range(GH):
                            last = stt(state[d][:, h, :], state[d][:, h, :], gexp[d][:, 4 + h:5 + h],
                                       b[:, h * P:(h + 1) * P], ALU.mult, ALU.add)
                        last.then_inc(dve_emptied, 1)
                dve.wait_ge(osq_ready, 3 * l + 3)
                inverse_root(flat(orr[:, 1:3, :]), flat(oss[:, 1:3, :]), 1.0 / GD, orr_ready)
                gated(1, flat(gb[0][10]))

                dve.wait_ge(act_emptied, job["gate", l, 1, 1, 1])
                for j in range(N_OUT):
                    for t in range(TILES):
                        b = filled("wout", l, j, t)
                        if j or t == 2:
                            dve.wait_ge(x_half, 3 * l + min(3 * j + t - 1, 3))
                        if (j, t) == (1, 2):
                            dve.wait_ge(x_ready, 6 * l + 1)
                        part = x[:, t, j * 512:(j + 1) * 512]
                        tt(silu_a[:, (3 * j + t) % 2, :], b[:], gate1[STREAM[t]][:, j * 512:(j + 1) * 512]).then_inc(dve_emptied, 1)
                        dve.wait_ge(dve_emptied, job["wout", l, j, t])
                        tt(part, part, silu_a[:, (3 * j + t) % 2, :], ALU.add).then_inc(x_ready if j else x_half, 1)
                        if j:
                            token_scales(l, 2, t, t + 1)
                modulated(2)

                dve.wait_ge(logits_full, 3 * l + 3)
                link(tt(lg, bank[3][:, 0:60].rearrange("p (t n) -> p t n", t=TILES), heads(b_rt[:, l, :], TILES), ALU.add))

                def best(one_hot, top, values):
                    link(vec.reduce_max(top, values, AX))
                    link(tt(one_hot, values, over(top, 4), ALU.is_equal))
                    link(tt(one_hot, one_hot, heads(tab("first"), TILES)))
                    link(vec.reduce_max(t3, one_hot, AX))
                    link(tt(one_hot, one_hot, over(t3, 4), ALU.is_equal))

                best(oh_g, m_g, lg[:, :, 0:4])
                lg16 = lg[:, :, 4:20].rearrange("p t (g j) -> p t g j", g=4)
                t16v = t16.rearrange("p t (g j) -> p t g j", g=4)
                link(tt(t16v, lg16, oh_g.unsqueeze(3).broadcast_to([P, TILES, 4, 4])))
                link(vec.reduce_sum(el, t16.rearrange("p t (g j) -> p t j g", g=4), AX))
                best(oh1, m_1, el)
                link(stt(el, oh1, -BIG, el, ALU.mult, ALU.add))
                best(oh2, m_2, el)
                tt(r_exp[:, :, 0:4], lg[:, :, 0:4], over(m_g, 4), ALU.subtract)
                tt(r_exp[:, :, 4], m_2, m_1, ALU.subtract).then_inc(router_x, 1)
                for c_, oh in enumerate((oh1, oh2)):
                    for t in range(TILES):
                        ins = tt(choice[:, t, c_, :].rearrange("p (g j) -> p g j", g=4), over(oh_g[:, t, :], 4),
                                 heads(oh[:, t, :], 4))
                link(ins)
                tt(chosen, choice[:, :, 0, :], choice[:, :, 1, :], ALU.add).then_inc(routed, 1)
                b = filled("place", l)
                vec.reduce_max(t1, b[:, 48:64], AX)
                stt(place, b[:, 0:48].rearrange("p (t n) -> p t n", t=TILES), 1.0, chosen, ALU.add,
                    ALU.mult).then_inc(dve_emptied, 1)
                dve.wait_ge(dve_emptied, job["place", l])
                vec.tensor_copy(most[:], t1[0:1, :]).then_inc(counted, 1)

                def lists(s, first, offset):
                    def link(ins):
                        ins.then_inc(s["step"], 1)
                        dve.wait_ge(s["step"], n(s["step"]))

                    link(ts(shifted, place, -float(offset + 1), op0=ALU.add))
                    def take_list(group):
                        dve.wait_ge(s["list_full"], first // 4 + group + 1)
                        link(vec.tensor_copy(pair_f, bank[6 + group % 2][:, 0:8]))
                        pf = pair_f.rearrange("p (e c) -> p e c", c=2)
                        stt(idx[:, 4 * group:4 * group + 4], pf[:, :, 1], float(P), pf[:, :, 0],
                            ALU.mult, ALU.add).then_inc(s["list_taken"], 1)
                        dve.wait_ge(s["list_taken"], first // 4 + group + 1)

                    for group in range(4):
                        for t in range(TILES):
                            ins = tt(sel[group % 2][:, t, :, :], heads(tab("slot"), 4),
                                     over(shifted[:, t, 4 * group:4 * group + 4], P), ALU.is_equal)
                        ins.then_inc(s["sel"], 1)
                        if group:
                            take_list(group - 1)
                    take_list(3)

                lists(es, l * EXPERTS, 0)
                dve.wait_ge(router_e, l + 1)
                link(vec.reduce_sum(t3, r_exp[:, :, 0:4], AX))
                link(vec.reciprocal(t3, t3))
                link(ts(m_1, r_exp[:, :, 4], 1.0, op0=ALU.add))
                link(vec.reciprocal(m_1, m_1))
                link(tt(w_tok[:, :, 0], t3, m_1))
                link(tt(w_tok[:, :, 1], w_tok[:, :, 0], r_exp[:, :, 4]))
                link(stt(t16, heads(tab("row0"), TILES), float(CAP), place, ALU.mult, ALU.add))
                for again in range(1, OVER + 1):
                    link(ts(shifted, place, float(again * CAP + 1), float((EXPERTS - 1) * CAP), ALU.is_ge, ALU.mult))
                    link(tt(t16, t16, shifted, ALU.add))
                for c_ in range(2):
                    link(tt(choice[:, :, c_, :], choice[:, :, c_, :], t16))
                    link(vec.reduce_sum(rowf[:, :, c_], choice[:, :, c_, :], AX))
                link(ts(idx_row[:], rowf, -1.0, op0=ALU.add))

                def run_experts(s, first):
                    def product(e, j, first_ever=False):
                        dve.wait_ge(s["silu"], e + 1)
                        dve.wait_ge(s["b_full"], e + 1)
                        if not first_ever:
                            dve.wait_ge(s["hTp"], e - 1)
                        tt(h_e[:, j, :], silu_a[:, j, :], bank[4 + j][:]).then_inc(s["h"], 1)

                    def result(e, j, pair, first_ever=False):
                        for half in range(2):
                            dve.wait_ge(s["y_full"], e * 2 + half + 1)
                            if not first_ever:
                                dve.wait_ge(s["y_stored"][j], 16 * pair)
                            vec.tensor_copy(y_e[:, j, half * 512:(half + 1) * 512], bank[6 + half][:]).then_inc(s["y"], 1)

                    pair = first // 2
                    product(first, 0, first == 0)
                    product(first + 1, 1, first == 0)
                    result(first, 0, pair, first == 0)

                    def two_experts(i, first_ever=False):
                        e = i * 2 + first
                        product(e, 0)
                        result(e - 1, 1, i + (pair - 1), first_ever)
                        product(e + 1, 1)
                        result(e, 0, i + pair)

                    two_experts(1, first == 0)
                    with dve.Fori(2, EXPERTS // 2) as i:
                        two_experts(i)
                    result(first + EXPERTS - 1, 1, pair + EXPERTS // 2 - 1)

                run_experts(es, l * EXPERTS)
                top = dve.value_load(most[0:1, 0:1])
                with dve.If(top > CAP):
                    for again in range(OVER):
                        if again:
                            dve.wait_ge(spare[l]["y_stored"][1], 16 * again * EXPERTS // 2)
                        else:
                            dve.wait_ge(es["y_stored"][1], 16 * (l + 1) * EXPERTS // 2)
                        lists(spare[l], again * EXPERTS, (again + 1) * CAP)
                        run_experts(spare[l], again * EXPERTS)

                for t in range(TILES + 1):
                    if t < TILES:
                        dve.wait_ge(combine_a, 3 * l + t + 1)
                        a = y_first[:, t, :]
                        stt(a, y_second[:, t, :], w_tok[:, t, 1:2], a, ALU.mult, ALU.add).then_inc(combine_b, 1)
                    if t:
                        dve.wait_ge(combine_c, 3 * l + t)
                        tt(x[:, t - 1, :], x[:, t - 1, :], y_first[:, t - 1, :], ALU.add).then_inc(x_ready, 1)

        @block.gpsimd
        def _(pool):
            n = Counts()
            gp = nc.gpsimd

            def link(ins):
                ins.then_inc(pool_step, 1)
                pool.wait_ge(pool_step, n(pool_step))

            def tt(out, a, b, op=ALU.mult):
                return gp.tensor_tensor(out, a, b, op)

            pool.wait_ge(consts_in, 16)
            for l in range(DEPTH):
                if l:
                    pool.wait_ge(x_ready, 6 * l)
                pool.dma_start(k_past, cache_k[0, l].rearrange("s h d -> s (h d)")).then_inc(past_in, 16)
                pool.dma_start(v_past, cache_v[0, l].rearrange("s h d -> s (h d)")).then_inc(past_in, 16)
                gp.memset(conv_in, 0.0).then_inc(pads_ready, 1)
                pool.wait_ge(zn_ready, 6 * l + 4)
                pool.dma_start(new_k[0, l].rearrange("s h d -> s (h d)"), z_k[:, 0, :]).then_inc(kv_stored, 16)
                pool.wait_ge(act_emptied, job["win", l, 2, 0])
                pool.dma_start(new_v[0, l].rearrange("s h d -> s (h d)"), v_sb[:, 0, :]).then_inc(kv_stored, 16)
                pool.wait_ge(kv_stored, 32 * (l + 1))
                def mask_bias(lot):
                    h4 = lot % 2
                    pool.wait_ge(bias_in[h4], 128 * (2 * l + lot // 2 + 1))
                    tt(bias[:, h4], bias[:, h4], heads(tab("window").rearrange("p r n -> p (r n)"), 4),
                       ALU.add).then_inc(bias_ready, 1)

                def squared(t):
                    qk = gq[:, t, 0:2].rearrange("p s h d -> p (s h) d")
                    tt(sq8, qk, qk).then_inc(sq_ready, 1)

                def lengths_and_turn(t):
                    qk = gq[:, t, 0:2].rearrange("p s h d -> p (s h) d")
                    pool.wait_ge(qr_ready, 3 * l + t + 1)
                    ins = tt(qk, qk, over(qr[:, t, :], GD))
                    if t:
                        link(ins)
                        v = qk.rearrange("p h (a b n) -> p h a b n", a=2, b=2)
                        x1, x2 = v[:, :, :, 0, :], v[:, :, :, 1, :]
                        cos_, sin_ = (tab(k)[:, t - 1].unsqueeze(1).broadcast_to([P, 8, 2, 32]) for k in ("cos", "sin"))
                        tt(turn[:, 0], x1, cos_)
                        tt(turn[:, 1], x2, sin_)
                        link(tt(turn[:, 2], x1, sin_))
                        link(tt(x1, turn[:, 0], turn[:, 1], ALU.subtract))
                        link(tt(turn[:, 0], x2, cos_))
                        ins = tt(x2, turn[:, 2], turn[:, 0], ALU.add)
                    ins.then_inc(gq_normed, 1)
                    pool.wait_ge(gq_normed, 3 * l + t + 1)
                    if t + 1 < TILES:
                        squared(t + 1)

                mask_bias(0)
                mask_bias(1)
                pool.wait_ge(act_emptied, job["conv_back", l, 11])
                squared(0)
                for t in range(TILES):
                    pool.wait_ge(act_emptied, job["win", l, 6, t])
                    zg_t = zg[:, t, :].rearrange("p (h n) -> p h n", h=GH)
                    tt(zg_t, zg_t, heads(gdn_g[:, l, :], GH)).then_inc(zg_scaled, 1)
                lengths_and_turn(0)
                lengths_and_turn(1)
                mask_bias(2)
                mask_bias(3)
                lengths_and_turn(2)

                pool.wait_ge(for_act, job["o_na", l, 2])
                for d in range(2):
                    gp.memset(state[d], 0.0).then_inc(state_zero, 1)
                pool.wait_ge(gates_ready, l + 1)
                incl = [tab("le"), tab("ge")]
                for step in range(3):
                    for d in range(2):
                        t = CHUNKS[step][d]
                        if step:
                            pool.wait_ge(for_dve, job["kv", l, step - 1, d])
                        tt(gb[d][0], heads(incl[d], GH), over(decay[:, t, 4 * d:4 * d + 4], P)).then_inc(decay_rhs, 1)
                    for d in range(2):
                        t = CHUNKS[step][d]
                        tt(gb[d][7], gq[:, t, 2], over(beta[:, t, 4 * d:4 * d + 4], GD))
                        pool.wait_ge(gexp_ready, 6 * l + 2 * step + d + 1)
                        tt(gb[d][6], gq[:, t, 1], over(gexp[d][:, 8:12], GD)).then_inc(pool_scaled, 1)
                    for level in range(LEVELS):
                        for d in range(2):
                            if level == 0:
                                pool.wait_ge(dve_emptied, job["kk", l, step, d])
                            elif level == 1:
                                pool.wait_ge(dve_emptied, job["t0", l, step, d])
                            else:
                                pool.wait_ge(for_act, job["at", l, step, level - 1, d])
                            tt(gb[d][0], gb[d][10], heads(tab("levels")[:, d, level, :], GH)).then_inc(lvl_ready, 1)

                pool.wait_ge(orr_ready, l + 1)
                acc3 = o_acc[:, 1, :].rearrange("p (h n) -> p h n", h=GH)
                link(tt(acc3, acc3, over(orr[:, 2, :], GD)))
                tt(flat(gb[1][10]), o_acc[:, 1, :], zg[:, 2, :]).then_inc(og2_ready, 1)

                for t in range(TILES):
                    pool.wait_ge(act_emptied, job["tok", l, t, 1])
                    pool.dma_start(tok_dram[t * P:(t + 1) * P, :], tok_sb[:, t, :]).then_inc(tok_stored, 16)
                pool.wait_ge(tok_stored, 48 * (l + 1))

                def run_experts(s, first):
                    pool.wait_ge(s["list_taken"], first // 4 + 1)

                    def gather(e, rel, j, first_ever=False):
                        if not first_ever:
                            pool.wait_ge(s["transposed"], e * 2 - 2)
                        gp.tensor_copy(idx_now[:, j:j + 1], idx[:, bass.ds(rel, 1)]).then_inc(s["idx_copied"], 1)
                        pool.wait_ge(s["idx_copied"], e + 1)
                        pool.sem_inc(s["gathering"])
                        pool.indirect_dma_start(
                            out=x_e[:, j, :], out_offset=None, in_=tok_dram,
                            in_offset=bass.IndirectOffsetOnAxis(ap=idx_now[:, j:j + 1], axis=0)).then_inc(s["gathered"][j], 16)

                    gather(first, 0, 0, first == 0)
                    gather(first + 1, 1, 1, first == 0)
                    pool.wait_ge(s["list_taken"], first // 4 + 4)
                    with pool.Fori(1, EXPERTS // 2) as i:
                        gather(i * 2 + first, i * 2, 0)
                        gather(i * 2 + (first + 1), i * 2 + 1, 1)

                run_experts(es, l * EXPERTS)
                for b in range(2):
                    pool.wait_ge(es["y_stored"][b], 16 * (l + 1) * EXPERTS // 2)

                def gather_rows(rows_):
                    for t in range(TILES):
                        for c_, dst in enumerate((y_first, y_second)):
                            pool.indirect_dma_start(
                                out=dst[:, t, :], out_offset=None, in_=expert_dram[0:rows_, :],
                                in_offset=bass.IndirectOffsetOnAxis(ap=idx_row[:, t, c_:c_ + 1], axis=0)
                            ).then_inc(y_in[t], 16)

                pool.wait_ge(counted, l + 1)
                top = pool.value_load(most[0:1, 0:1])
                with pool.If(top > CAP):
                    for again in range(OVER):
                        run_experts(spare[l], again * EXPERTS)
                    for b in range(2):
                        pool.wait_ge(spare[l]["y_stored"][b], 16 * OVER * EXPERTS // 2)
                    gather_rows((1 + OVER) * EXPERTS * CAP)
                with pool.If(top < CAP + 1):
                    gather_rows(EXPERTS * CAP)
                for t in range(TILES):
                    pool.wait_ge(combine_b, 3 * l + t + 1)
                    tt(y_first[:, t, :], y_first[:, t, :], gate2[:, STREAM[t], :]).then_inc(combine_c, 1)


_INS = ["x_prompt", "x_sample", "c", "cache_k", "cache_v", "state_ssm", "c_ctx", "ada_w", "ada_b", "norm1_g",
        "norm2_g", "w_in", "w_out", "na_qn_g", "na_kn_g", "na_rpb", "gdn_conv_w", "gdn_a_log", "gdn_dt_bias",
        "gdn_norm_g", "moe_w_rg", "moe_b_rg", "moe_w_re", "moe_b_re", "moe_w1", "moe_w3", "moe_w2"]
_OUTS = [(1, CTX, D), (1, LAT, D), (1, DEPTH, CTX, HEADS, HD), (1, DEPTH, CTX, HEADS, HD),
         (1, DEPTH, 2, GH, GD, GD)]


def kernel(**inputs):
    import concourse.bacc as _bacc
    from concourse.bass_utils import run_bass_kernel_spmd as _run

    nc = _bacc.Bacc("TRN2", target_bir_lowering=False, num_devices=1)
    where, tables = constants()
    arrays, args = {}, []
    for name in _INS:
        a = np.ascontiguousarray(inputs[name])
        arrays[f"in_{name}_dram"] = a
        args.append(nc.dram_tensor(f"in_{name}_dram", a.shape, mybir.dt.from_np(a.dtype), kind="ExternalInput").ap())
    arrays["in_tables_dram"] = tables
    args.append(nc.dram_tensor("in_tables_dram", tables.shape, F32, kind="ExternalInput").ap())
    for i, shape in enumerate(_OUTS):
        args.append(nc.dram_tensor(f"out_{i}_dram", shape, F32, kind="ExternalOutput").ap())
    program(nc, *args, where)
    r = _run(nc, [arrays], core_ids=[0])
    return tuple(r.results[0][f"out_{i}_dram"] for i in range(len(_OUTS)))
```
